# Optimizing a Trainium2 kernel written in Bass

```python
import math
import jax, jax.numpy as jnp
from jax import lax
import numpy as np

D_MODEL = 1024
BATCH = 1
SEQ = 1024
DEPTH = 1

HEAD_DIM = 64
POOL_WINDOWS = (2, 4, 8, 16)
POOL_GROUP_DIM = D_MODEL // 16
POOL_DIM = len(POOL_WINDOWS) * POOL_GROUP_DIM
ATTN_GROUPS = ((128, 1), (512, 4), (2048, 16))
N_ATTN_HEADS = (D_MODEL - POOL_DIM) // HEAD_DIM
HEADS_PER_GROUP = N_ATTN_HEADS // len(ATTN_GROUPS)
ATTN_DIM = N_ATTN_HEADS * HEAD_DIM
D_MIX = POOL_DIM + ATTN_DIM
D_IN = POOL_DIM + 3 * ATTN_DIM
D_FF = 64 * int(math.ceil(8 * D_MODEL / (3 * 64)))
RMS_EPS = 1e-6

kernel_name = "hymba_pool_dilated_alibi_macaron"

def alibi_slopes():
    s = np.array([2.0 ** (-8.0 * (i + 1) / N_ATTN_HEADS) for i in range(N_ATTN_HEADS)], np.float32)
    return jnp.asarray(s)

def rmsnorm(x, g):
    xf = x.astype(jnp.float32)
    y = xf * lax.rsqrt(jnp.mean(xf * xf, axis=-1, keepdims=True) + RMS_EPS)
    return (y * g.astype(jnp.float32)).astype(x.dtype)

def swiglu(h, w_gate, w_up, w_down):
    return (jax.nn.silu(h @ w_gate) * (h @ w_up)) @ w_down

def pool_mixer(u, w_lin, scale):
    B, S, _ = u.shape
    G = len(POOL_WINDOWS)
    uf = u.astype(jnp.float32).reshape(B, S, G, POOL_GROUP_DIM)
    csum = jnp.concatenate([jnp.zeros((B, 1, G, POOL_GROUP_DIM), jnp.float32),
                            jnp.cumsum(uf, axis=1)], axis=1)
    t = jnp.arange(S)
    outs = []
    for g, w in enumerate(POOL_WINDOWS):
        lo = jnp.clip(t - w // 2, 0, S)
        hi = jnp.clip(t - w // 2 + w, 0, S)
        cg = csum[:, :, g]
        win_sum = jnp.take(cg, hi, axis=1) - jnp.take(cg, lo, axis=1)
        mean = win_sum / (hi - lo).astype(jnp.float32)[None, :, None]
        outs.append(mean - uf[:, :, g])
    y = jnp.stack(outs, axis=2).astype(u.dtype)
    y = jnp.einsum('bsgc,gce->bsge', y, w_lin)
    return y.reshape(B, S, POOL_DIM) * scale

def dilated_window_attention(q, k, v, window, dilation, slopes):
    B, S, H, Dh = q.shape
    n_side = (window // 2) // dilation
    blk = n_side
    L = S // dilation
    nb = -(-L // blk)
    Lp = nb * blk

    def to_sub(a):
        return a.reshape(B, L, dilation, H, Dh).transpose(0, 2, 1, 3, 4).reshape(B * dilation, L, H, Dh)

    def windows(a):
        a = jnp.pad(to_sub(a), ((0, 0), (blk, Lp - L + blk), (0, 0), (0, 0)))
        a = a.reshape(-1, nb + 2, blk, H, Dh)
        return jnp.concatenate([a[:, :-2], a[:, 1:-1], a[:, 2:]], axis=2)

    qs = jnp.pad(to_sub(q), ((0, 0), (0, Lp - L), (0, 0), (0, 0))).reshape(-1, nb, blk, H, Dh)
    kw, vw = windows(k), windows(v)

    rel = jnp.arange(3 * blk)[None, :] - blk - jnp.arange(blk)[:, None]
    key_idx = (jnp.arange(nb)[:, None] - 1) * blk + jnp.arange(3 * blk)[None, :]
    valid = (jnp.abs(rel) <= n_side)[None] & ((key_idx >= 0) & (key_idx < L))[:, None, :]
    dist = (jnp.abs(rel) * dilation).astype(jnp.float32)
    bias = -slopes.astype(jnp.float32)[:, None, None] * dist[None]

    s = jnp.einsum('znqhd,znkhd->znhqk', qs, kw).astype(jnp.float32) * (Dh ** -0.5)
    s = jnp.where(valid[None, :, None], s + bias[None, None], -jnp.inf)
    m = jnp.max(s, axis=-1, keepdims=True)
    p = jnp.exp(s - m)
    den = jnp.sum(p, axis=-1)
    o = jnp.einsum('znhqk,znkhd->znqhd', p, vw.astype(jnp.float32))
    den_t = jnp.swapaxes(den, 2, 3)
    o = o / den_t[..., None]
    lse = jnp.swapaxes(m[..., 0], 2, 3) + jnp.log(den_t)

    def from_sub(a):
        a = a.reshape((B, dilation, Lp) + a.shape[3:])[:, :, :L]
        a = jnp.swapaxes(a, 1, 2)
        return a.reshape((B, S) + a.shape[3:])

    return from_sub(o), from_sub(lse)

def attention_mixer(q, k, v):
    B, S = q.shape[:2]
    slopes = alibi_slopes()
    outs, lses = [], []
    for gi, (window, dilation) in enumerate(ATTN_GROUPS):
        hs = slice(gi * HEADS_PER_GROUP, (gi + 1) * HEADS_PER_GROUP)
        o, lse = dilated_window_attention(q[:, :, hs], k[:, :, hs], v[:, :, hs],
                                          window, dilation, slopes[hs])
        outs.append(o)
        lses.append(lse)
    alpha = jax.nn.softmax(jnp.stack(lses, axis=0), axis=0)
    o = jnp.concatenate([outs[g] * alpha[g][..., None] for g in range(len(ATTN_GROUPS))], axis=2)
    return o.reshape(B, S, ATTN_DIM).astype(q.dtype)

def setup_inputs(seed: int = 0) -> dict:
    key = jax.random.key(seed)
    ks = jax.random.split(key, 20)
    f32 = jnp.float32

    def nrm(k, shape, fan_in):
        return jax.random.normal(k, shape, f32) * (fan_in ** -0.5)

    def gain(k, n):
        return 1.0 + 0.02 * jax.random.normal(k, (DEPTH, n), f32)

    return {
        "x": jax.random.normal(ks[0], (BATCH, SEQ, D_MODEL), f32),
        "g_ffn1_pre": gain(ks[1], D_MODEL),
        "w1_gate": nrm(ks[2], (DEPTH, D_MODEL, D_FF), D_MODEL),
        "w1_up": nrm(ks[3], (DEPTH, D_MODEL, D_FF), D_MODEL),
        "w1_down": nrm(ks[4], (DEPTH, D_FF, D_MODEL), D_FF),
        "g_ffn1_post": gain(ks[5], D_MODEL),
        "g_mix_pre": gain(ks[6], D_MODEL),
        "w_in": nrm(ks[7], (DEPTH, D_MODEL, D_IN), D_MODEL),
        "w_pool_lin": nrm(ks[8], (DEPTH, len(POOL_WINDOWS), POOL_GROUP_DIM, POOL_GROUP_DIM), POOL_GROUP_DIM),
        "pool_scale": gain(ks[9], POOL_DIM),
        "w_out": nrm(ks[10], (DEPTH, D_MIX, D_MODEL), D_MIX),
        "g_mix_post": gain(ks[11], D_MODEL),
        "g_ffn2_pre": gain(ks[12], D_MODEL),
        "w2_gate": nrm(ks[13], (DEPTH, D_MODEL, D_FF), D_MODEL),
        "w2_up": nrm(ks[14], (DEPTH, D_MODEL, D_FF), D_MODEL),
        "w2_down": nrm(ks[15], (DEPTH, D_FF, D_MODEL), D_FF),
        "g_ffn2_post": gain(ks[16], D_MODEL),
    }

def reference(x, g_ffn1_pre, w1_gate, w1_up, w1_down, g_ffn1_post, g_mix_pre, w_in,
              w_pool_lin, pool_scale, w_out, g_mix_post, g_ffn2_pre, w2_gate, w2_up,
              w2_down, g_ffn2_post):
    B, S, _ = x.shape
    for l in range(DEPTH):
        x = x + 0.5 * rmsnorm(swiglu(rmsnorm(x, g_ffn1_pre[l]), w1_gate[l], w1_up[l], w1_down[l]),
                              g_ffn1_post[l])
        h = rmsnorm(x, g_mix_pre[l])
        z = h @ w_in[l]
        u = z[..., :POOL_DIM]
        qkv = z[..., POOL_DIM:].reshape(B, S, 3, N_ATTN_HEADS, HEAD_DIM)
        a_pool = pool_mixer(u, w_pool_lin[l], pool_scale[l])
        a_attn = attention_mixer(qkv[:, :, 0], qkv[:, :, 1], qkv[:, :, 2])
        mix = jnp.concatenate([a_pool.astype(x.dtype), a_attn.astype(x.dtype)], axis=-1) @ w_out[l]
        x = x + rmsnorm(mix, g_mix_post[l])
        x = x + 0.5 * rmsnorm(swiglu(rmsnorm(x, g_ffn2_pre[l]), w2_gate[l], w2_up[l], w2_down[l]),
                              g_ffn2_post[l])
    return x


_drawn_inputs = setup_inputs


def setup_inputs(seed=0):
    import zlib

    import numpy as np

    out = dict(_drawn_inputs(seed))
    spreads = {}
    factors = {'g_ffn1_pre': 3.802,
     'g_ffn1_post': 5.631,
     'g_mix_pre': 3.698,
     'pool_scale': 12.003,
     'g_mix_post': 11.96,
     'g_ffn2_pre': 20.5,
     'g_ffn2_post': 36.563}
    for name, (base, spread) in spreads.items():
        noise = np.random.default_rng([zlib.crc32(name.encode()), seed]).standard_normal(out[name].shape)
        drawn = base * np.exp(spread * noise) if base else spread * noise
        out[name] = __import__('jax').numpy.asarray(drawn.astype(out[name].dtype))
    for name, factor in factors.items():
        out[name] = (out[name] * factor).astype(out[name].dtype)
    return out
```

```python
from contextlib import ExitStack

import numpy as np
import concourse.bass as bass
from concourse import mybir

F32 = mybir.dt.float32
F32R = mybir.dt.float32r
ALU = mybir.AluOpType
ACT = mybir.ActivationFunctionType

P = 128
SEQ, D = 1024, 1024
HALF = SEQ // 2
HT = HALF // P
DT = D // P
FF = 64 * -(-8 * D // (3 * 64))
FT = FF // P
TAIL = FF - FT * P
NFT = FT + 1
HEAD = 64
NGROUP, HPG = 3, 4
POOL_DIM = D // 4
POOL_WINDOWS = (2, 4, 8, 16)
DILATION = (1, 4, 16)
N_HEADS = NGROUP * HPG
SIDE = 64
RMS_EPS = 1e-6
QK_SCALE = HEAD ** -0.5
MASKED = -1e30
NT = SEQ // P
NTILES = NGROUP * NT
PAD = max(POOL_WINDOWS) // 2
POOL_STEPS = 2 + 6 * len(POOL_WINDOWS)

RAW_SLOTS, SPLIT_SLOTS = 4, 2
BLOCK = 4
GU_UNITS = 2 * FT + 1
DOWN_UNITS = NFT
IN_UNITS = (POOL_DIM + 3 * N_HEADS * HEAD) // P
OUT_UNITS = DT
_sizes = [GU_UNITS, DOWN_UNITS] * 2 + [IN_UNITS] * 2 + [OUT_UNITS] * 2 + [GU_UNITS, DOWN_UNITS] * 2
_starts = [sum(_sizes[:n]) for n in range(len(_sizes) + 1)]
GU_U0 = [_starts[0], _starts[2], _starts[8], _starts[10]]
DOWN_U0 = [_starts[1], _starts[3], _starts[9], _starts[11]]
IN_U0 = [_starts[4], _starts[5]]
OUT_U0 = [_starts[6], _starts[7]]
UNITS = _starts[-1]
TAIL_UNITS = [u0 + GU_UNITS - 1 for u0 in GU_U0]
Y_OF_FFN, Y_OF_MIX = [0, 1, 4, 5], [2, 3]

LO_CREDIT, USED_CREDIT, H_CREDIT, Z_CREDIT = RAW_SLOTS, SPLIT_SLOTS, 2, 4

ACC_ORDER = (2, 3, 0, 1)


def loaded_count(u0, t, k):
    u = u0 + k
    if isinstance(t, int):
        t, u = 0, u + BLOCK * t
    tails = sum(1 for v in TAIL_UNITS if v <= u and v % RAW_SLOTS == u % RAW_SLOTS)
    return (t + u // RAW_SLOTS + 1 + tails) * 16


def natural(ap, g, c):
    if g == 0:
        return ap[:, c * HALF:(c + 1) * HALF]
    d = DILATION[g]
    n = d // 2
    return ap.rearrange("p (l r) -> p r l", r=d)[:, c * n:(c + 1) * n, :]


def as_permuted(ap, g):
    if g == 0:
        return ap
    return ap.rearrange("p (r l) -> p r l", r=DILATION[g] // 2)


def layer_program(nc, io, out, xs1, xs2):
    ctx = ExitStack()
    with ctx:
        def sb(name, shape, dt=F32):
            return ctx.enter_context(nc.sbuf_tensor(name, shape, dt))

        def sem(name):
            return ctx.enter_context(nc.semaphore(name))

        raw = sb("raw", [P, RAW_SLOTS, D])
        w_hi = sb("w_hi", [P, SPLIT_SLOTS, D], F32R)
        w_lo = sb("w_lo", [P, SPLIT_SLOTS, D], F32R)
        y = sb("y", [P, HT, D])
        x_tile = sb("x_tile", [P, D])
        xn = sb("xn", [P, D])
        g_post = sb("g_post", [P, D])
        g_pre = sb("g_pre", [P, D])
        ident = sb("ident", [P, P])
        neg_half = sb("neg_half", [P, 1])
        ss1 = sb("ss1", [P, 1])
        ss2 = sb("ss2", [P, 1])
        ms1 = sb("ms1", [P, 1])
        ms2 = sb("ms2", [P, 1])
        r1 = sb("r1", [P, 1])
        r2 = sb("r2", [P, 1])
        m_max = sb("m_max", [P, NTILES, HPG])
        m_neg = sb("m_neg", [P, NTILES, HPG])
        den = sb("den", [P, NTILES, HPG])
        coef = sb("coef", [P, NTILES * HPG])
        edge = sb("edge", [P, 2, 2 * PAD])
        pool_scale = sb("pool_scale", [P, 2])
        sel_w = sb("sel_w", [P, 2, P])

        with ExitStack() as first:
            x_hi = [first.enter_context(nc.sbuf_tensor(f"x_hi{n}", [P, DT, HALF], F32R)) for n in (0, 1)]
            x_lo = [first.enter_context(nc.sbuf_tensor(f"x_lo{n}", [P, DT, HALF], F32R)) for n in (0, 1)]
        with ExitStack() as second:
            v_nat = second.enter_context(nc.sbuf_tensor("v_nat", [P, NGROUP, NT, HPG * HEAD], F32))
            v_mid = second.enter_context(nc.sbuf_tensor("v_mid", [P, NT - 1, HPG * HEAD], F32))
            o_all = second.enter_context(nc.sbuf_tensor("o_all", [P, NTILES, HPG * HEAD], F32))
            probs = second.enter_context(nc.sbuf_tensor("probs", [P, 2, HPG, 2 * P], F32))
        sb("region1", [P, 2 * 2 * DT * HALF])

        with ExitStack() as first:
            h_all = first.enter_context(nc.sbuf_tensor("h_all", [P, NFT, HALF], F32))
            hs_hi = first.enter_context(nc.sbuf_tensor("hs_hi", [P, SPLIT_SLOTS, HALF], F32R))
            hs_lo = first.enter_context(nc.sbuf_tensor("hs_lo", [P, SPLIT_SLOTS, HALF], F32R))
            sil = first.enter_context(nc.sbuf_tensor("sil", [P, 2, HALF], F32))
            y_b = first.enter_context(nc.sbuf_tensor("y_b", [P, HT, D], F32))
        with ExitStack() as second:
            qk = second.enter_context(nc.sbuf_tensor("qk", [P, 12, SEQ], F32))
            vT = second.enter_context(nc.sbuf_tensor("vT", [P, 6, SEQ], F32))
        with ExitStack() as third:
            mixT = third.enter_context(nc.sbuf_tensor("mixT", [P, DT, SEQ], F32))
            win_a = third.enter_context(nc.sbuf_tensor("win_a", [P, 2, PAD + SEQ], F32))
            win_b = third.enter_context(nc.sbuf_tensor("win_b", [P, 2, PAD + SEQ], F32))
            stat = third.enter_context(nc.sbuf_tensor("stat", [HPG, 2, NGROUP, SEQ], F32))
        with ExitStack() as fourth:
            fourth.enter_context(nc.sbuf_tensor("under_bias", [P, 12, SEQ], F32))
            bias = fourth.enter_context(nc.sbuf_tensor("bias", [P, 5 * HPG * 2 * P + HPG * P], F32))
        sb("region2", [P, DT * SEQ + 4 * (PAD + SEQ) + 2 * NGROUP * SEQ])
        u_pool = y[:, 0:2, :]
        probsT = y[:, 2:4, :].rearrange("p s (c n) -> p s c n", c=2)
        m_all_max = probs[0:HPG, 0, :, :].rearrange("p a b -> p (a b)")
        den_sum = probs[0:HPG, 1, :, :].rearrange("p a b -> p (a b)")

        ps = ctx.enter_context(nc.psum_tensor("ps", [P, 8, 512], F32))
        junk = ps[:, 6:8, :].rearrange("p a b -> p (a b)")

        w_loaded = [sem(f"w_loaded{n}") for n in range(RAW_SLOTS)]
        hi_done = sem("hi_done")
        lo_done = sem("lo_done")
        used = sem("used")
        sil_done = sem("sil_done")
        h_done = sem("h_done")
        y_act = sem("y_act")
        y_dve = sem("y_dve")
        ident_in = sem("ident_in")
        const_in = sem("const_in")
        bias_in = sem("bias_in")
        g_in = sem("g_in")
        y_in = [sem(f"y_in{n}") for n in range(HT)]
        y_half1_in = sem("y_half1_in")
        sq1_done = sem("sq1_done")
        ms1_done = sem("ms1_done")
        z_done = sem("z_done")
        x_in = sem("x_in")
        xnew_done = sem("xnew_done")
        x_out = sem("x_out")
        sq2_done = sem("sq2_done")
        ms2_done = sem("ms2_done")
        r2_done = sem("r2_done")
        xn_done = sem("xn_done")
        xT_done = sem("xT_done")
        xhi_done = sem("xhi_done")
        xlo_done = sem("xlo_done")
        z_evac = sem("z_evac")
        tr_done = sem("tr_done")
        tr_act = sem("tr_act")
        tr_dve = sem("tr_dve")
        s_done = sem("s_done")
        max_part = sem("max_part")
        smax_done = sem("smax_done")
        exp_done = sem("exp_done")
        pT_done = sem("pT_done")
        pT_act = sem("pT_act")
        pT_dve = sem("pT_dve")
        pv_done = sem("pv_done")
        o_done = sem("o_done")
        stat_step = sem("stat_step")
        stat_exp = sem("stat_exp")
        coef_done = sem("coef_done")
        scaled = sem("scaled")
        scaled_dve = sem("scaled_dve")
        pool_step = sem("pool_step")
        pool_lin = sem("pool_lin")
        mix_pool = sem("mix_pool")
        zeroed = sem("zeroed")

        def wait(eng, s, n):
            if not isinstance(n, int) or n > 0:
                eng.wait_ge(s, n)

        x_in_dram = io["x"]
        JOBS = [
            dict(half=0, y=y, Q0=0), dict(half=1, y=y, Q0=4),
            dict(half=0, y=y, src=x_in_dram, dst=xs1, d=0, junk_d=0, P0=0, Q0=8),
            dict(half=1, y=y, src=x_in_dram, dst=xs1, d=1, junk_d=1, P0=4, Q0=12),
            dict(half=0, y=y, src=xs1, dst=xs2, d=2, junk_d=3, P0=8, Q0=16),
            dict(half=1, y=y_b, src=xs1, dst=xs2, d=3, junk_d=3, P0=12, Q0=20),
            dict(half=0, y=y, src=xs2, dst=out, d=4, junk_d=4, P0=16),
            dict(half=1, y=y, src=xs2, dst=out, d=5, junk_d=5, P0=20),
        ]
        G_COUNT = [16, 16, 48, 48, 80, 80, 96, 96]

        TR_V, TR_STAT, TR_COEF = 0, 16, 28
        TR_O = 29

        def tr_copied(eng, b):
            eng.wait_ge(tr_act if b % 2 == 0 else tr_dve, b // 2 + 1)

        def copy_v(copy, b):
            bank = ps[:, 4 + b % 4, :]
            if b < 12:
                g, c = divmod(b, 4)
                copy(b, v_nat[:, g, 2 * c:2 * c + 2, :].rearrange("p a b -> p (a b)"), bank)
            else:
                c = b - 12
                n = 2 if c < 3 else 1
                copy(b, v_mid[:, 2 * c:2 * c + n, :].rearrange("p a b -> p (a b)"), bank[:, 0:n * HPG * HEAD])

        def copy_stat(copy, b):
            s, g, c = (b - TR_STAT) // 6, (b - TR_STAT) % 6 // 2, b % 2
            copy(b, natural(stat[:, s, g, :], g, c), as_permuted(ps[0:HPG, 4 + b % 4, :], g))

        def copy_coef(copy):
            copy(TR_COEF, coef[:, :], ps[:, 4 + TR_COEF % 4, 0:NTILES * HPG])

        def copy_o(copy, b):
            g, w, c = (b - TR_O) // 4, (b - TR_O) // 2 % 2, (b - TR_O) % 2
            copy(b, natural(mixT[:, 2 + 2 * g + w, :], g, c), as_permuted(ps[:, 4 + b % 4, :], g))

        def scale_out(eng, g):
            o = o_all[:, g * NT:(g + 1) * NT, :].rearrange("p n (h e) -> p (n h) e", e=HEAD)
            c = coef[:, g * NT * HPG:(g + 1) * NT * HPG].rearrange("p (a o) -> p a o", o=1)
            return eng.tensor_tensor(o, o, c.to_broadcast([P, NT * HPG, HEAD]), ALU.mult)

        block = ctx.enter_context(nc.Block())

        @block.sync
        def _(sp):
            def load(u0, t, k, dst_cols, src):
                sp.wait_ge(lo_done, t * BLOCK + (u0 + k - RAW_SLOTS + 1 + LO_CREDIT))
                slot = (u0 + k) % RAW_SLOTS
                for cols, s in zip(dst_cols, src):
                    sp.dma_start(cols(raw[:, slot, :]), s).then_inc(w_loaded[slot], 16)

            def columns(w, start, n=P):
                return w.rearrange("(a p) f -> p a f", p=P)[:, :, bass.ds(start, n)]

            def col_tile(ap):
                return ap.rearrange("p (a f) -> p a f", a=DT)

            def gate_up(p, u0):
                gate, up = io[f"w{p}_gate"], io[f"w{p}_up"]

                def tile(t, k):
                    load(u0, t, k, [col_tile], [columns((gate, up)[k % 2], t * 2 * P + k // 2 * P)])

                with sp.Fori(0, FT // 2) as t:
                    for k in range(BLOCK):
                        tile(t, k)
                for k in range(2):
                    tile(FT // 2, k)
                load(u0, FT // 2, 2, [lambda ap: col_tile(ap)[:, :, 0:TAIL], lambda ap: col_tile(ap)[:, :, TAIL:P]],
                     [columns(gate, FT * P, TAIL), columns(up, FT * P, TAIL)])

            def rows(w, u0, n, tail):
                def tile(t, k, count=P):
                    load(u0, t, k, [lambda ap: ap[0:count, :]], [w[bass.ds(t * BLOCK * P + k * P, count), :]])

                with sp.Fori(0, n // BLOCK) as t:
                    for k in range(BLOCK):
                        tile(t, k)
                for k in range(n % BLOCK):
                    tile(n // BLOCK, k, tail if k == n % BLOCK - 1 else P)

            sp.dma_start(y[:, 0, :], io["x"][0:P, :]).then_inc(y_in[0], 16)
            sp.dma_start(ident[:, :], io["ident"]).then_inc(ident_in, 16)
            for i in range(1, HT):
                sp.dma_start(y[:, i, :], io["x"][i * P:(i + 1) * P, :]).then_inc(y_in[i], 16)
            for ap, name in ((edge[:, :, :], "edge"), (pool_scale[:, :], "pool_scale")):
                sp.dma_start(ap, io[name]).then_inc(const_in, 16)
            sp.wait_ge(zeroed, 2)
            for n in range(len(POOL_WINDOWS)):
                a = (n % 2) * HEAD
                sp.dma_start(sel_w[a:a + HEAD, n // 2, a:a + HEAD], io["w_pool_lin"][n]).then_inc(const_in, 16)
            sp.wait_ge(xn_done, HT)
            sp.dma_start(y[:, :, :], io["x"][HALF:SEQ, :].rearrange("(i p) d -> p i d", p=P)).then_inc(y_half1_in, 16)
            for p in (0, 1):
                gate_up(1, GU_U0[p])
                rows(io["w1_down"], DOWN_U0[p], DOWN_UNITS, TAIL)
            for hf in (0, 1):
                def tile(t, k, col):
                    load(IN_U0[hf], t, k, [col_tile], [columns(io["w_in"], col)])

                with sp.Fori(0, 4) as t:
                    for k in range(BLOCK):
                        tile(t, k, t * BLOCK * P + k * P + POOL_DIM)
                for k in range(BLOCK):
                    tile(4, k, (4 * BLOCK + k) * P + POOL_DIM if k < 2 else (k - 2) * P)
            tr_copied(sp, TR_STAT - 2)
            tr_copied(sp, TR_STAT - 1)
            sp.dma_start(bias[:, :], io["bias"]).then_inc(bias_in, 16)
            for hf in (0, 1):
                rows(io["w_out"], OUT_U0[hf], OUT_UNITS, P)
            for p in (2, 3):
                gate_up(2, GU_U0[p])
                rows(io["w2_down"], DOWN_U0[p], DOWN_UNITS, TAIL)

        @block.scalar
        def _(act):
            act.sem_inc(z_evac, Z_CREDIT)

            def split(u0, t, k, src=None, ready=None):
                s = (u0 + k) % SPLIT_SLOTS
                act.wait_ge(w_loaded[(u0 + k) % RAW_SLOTS], loaded_count(u0, t, k))
                act.wait_ge(used, t * BLOCK + (u0 + k - SPLIT_SLOTS + 1 + USED_CREDIT))
                w = act.activation(w_hi[:, s, :], raw[:, (u0 + k) % RAW_SLOTS, :], ACT.Copy)
                if src is not None:
                    if ready is not None:
                        act.wait_ge(*ready)
                    w = act.activation(hs_hi[:, s, :], src, ACT.Copy)
                w.then_inc(hi_done, 1)

            def sq1(i, job):
                act.wait_ge(y_act, job["junk_d"] * HT + HT)
                act.wait_ge(y_dve, job["junk_d"] * HT + HT)
                if "Q0" not in job:
                    act.wait_ge(z_done, i + job["P0"])
                act.activation(junk, job["y"][:, bass.ds(i, 1), :].rearrange("p a b -> p (a b)"), ACT.Square,
                               accum_out=ss1[:, :]).then_inc(sq1_done, 1)

            def sq2(i, job):
                wait(act, ms2_done, i + job["Q0"])
                if "src" in job:
                    act.wait_ge(xnew_done, i + job["P0"] + 1)
                    src = x_tile[:, :]
                else:
                    act.wait_ge(y_in[i] if job["half"] == 0 else y_half1_in, 16)
                    src = y[:, bass.ds(i, 1), :].rearrange("p a b -> p (a b)")
                act.activation(junk, src, ACT.Square, accum_out=ss2[:, :]).then_inc(sq2_done, 1)

            def x_hi_part(i, job):
                act.wait_ge(xT_done, i + job["Q0"] + 1)
                for b in (0, 1):
                    dst = x_hi[job["half"]][:, 4 * b:4 * b + 4, bass.ds(i * P, P)]
                    a = act.activation(dst, ps[:, 4 + b, :].rearrange("p (a c) -> p a c", a=4), ACT.Copy)
                a.then_inc(xhi_done, 1)

            def silu(u0, t, k, f0, j_par, rows_in=slice(0, P), rows_out=slice(0, P)):
                act.wait_ge(used, t * BLOCK + (u0 + k + 1 + USED_CREDIT))
                act.wait_ge(h_done, t * 2 + (f0 + k // 2 - 1 + H_CREDIT))
                act.activation(sil[rows_out, j_par, :], ps[rows_in, 2 * j_par, :], ACT.Silu).then_inc(sil_done, 1)

            def gate_up(p, side=None):
                u0, f0 = GU_U0[p], NFT * p

                def blk(t, side):
                    for k in range(BLOCK):
                        split(u0, t, k + 2)
                        if side and k == 0 and "src" in side:
                            sq1(t, side)
                        if side and k == 1 and "Q0" in side:
                            sq2(t, side)
                        if k % 2 == 0:
                            silu(u0, t, k, f0, k // 2)
                        if side and k == 2 and "Q0" in side:
                            x_hi_part(t, side)

                with act.Fori(0, HT) as t:
                    blk(t, side)
                with act.Fori(HT, FT // 2) as t:
                    blk(t, None)
                T = FT // 2
                split(u0, T, 2)
                silu(u0, T, 0, f0, 0)
                split(DOWN_U0[p], 0, 0, h_all[:, 0, :], (h_done, f0 + 1 + H_CREDIT))
                silu(u0, T, 2, f0, 1, slice(0, TAIL), slice(TAIL, P))
                split(DOWN_U0[p], 0, 1, h_all[:, 1, :], (h_done, f0 + 2 + H_CREDIT))

            def evac_y(d, dst, last_unit):
                act.wait_ge(used, last_unit + 1 + USED_CREDIT)
                if d == Y_OF_FFN[3]:
                    act.wait_ge(xnew_done, JOBS[7]["P0"])
                for i in range(HT):
                    act.activation(dst[:, i, 0:512], ps[:, 2 * i, :], ACT.Copy).then_inc(y_act, 1)

            def down(p, nxt):
                u0, f0 = DOWN_U0[p], NFT * p

                def sp2(t, k):
                    src = h_all[:, bass.ds(t * BLOCK + k + 2, 1), :].rearrange("p a b -> p (a b)")
                    split(u0, t, k + 2, src, (h_done, t * BLOCK + (f0 + k + 3 + H_CREDIT)))

                with act.Fori(0, DOWN_UNITS // BLOCK) as t:
                    for k in range(BLOCK):
                        sp2(t, k)
                if nxt is not None:
                    split(nxt, 0, 0)
                    split(nxt, 0, 1)
                evac_y(Y_OF_FFN[p], y, u0 + DOWN_UNITS - 1)

            def project_in(hf, side):
                u0 = IN_U0[hf]
                for l in range(IN_UNITS):
                    t, k = l // BLOCK, l % BLOCK
                    if l + 2 < IN_UNITS:
                        split(u0, 0, l + 2)
                    elif hf == 0:
                        split(IN_U0[1], 0, l + 2 - IN_UNITS)
                    if side and t < HT:
                        if k == 0:
                            sq1(t, side)
                        if k == 1:
                            sq2(t, side)
                        if k == 2:
                            x_hi_part(t, side)
                    act.wait_ge(used, u0 + l + 1 + USED_CREDIT)
                    src = ps[:, l % 4, :]
                    if l >= 18:
                        dst = u_pool[:, l - 18, hf * HALF:(hf + 1) * HALF]
                    else:
                        dst = qk[:, l, :] if l < 12 else vT[:, l - 12, :]
                        d = DILATION[(l % 6) // 2]
                        n = HALF // d
                        if d == 1:
                            dst = dst[:, hf * HALF:(hf + 1) * HALF]
                        else:
                            dst = dst.rearrange("p (r l) -> p r l", r=d)[:, :, hf * n:(hf + 1) * n]
                            src = src.rearrange("p (l r) -> p r l", r=d)
                    act.activation(dst, src, ACT.Copy).then_inc(z_evac, 1)

            def tr_copy(b, dst, src):
                act.wait_ge(tr_done, b + 1)
                act.activation(dst, src, ACT.Copy).then_inc(tr_act, 1)

            def attention():
                for b in range(0, 16, 2):
                    copy_v(tr_copy, b)

                def exps(n):
                    act.wait_ge(smax_done, n + 1)
                    nk = P if n >= 2 * NT else 2 * P
                    for h in range(HPG):
                        a = act.activation(probs[:, n % 2, h, 0:nk], probs[:, n % 2, h, 0:nk], ACT.Exp,
                                           bias=m_neg[:, n, h:h + 1], accum_out=den[:, n, h:h + 1])
                    a.then_inc(exp_done, 1)

                exps(0)
                for n in range(NTILES):
                    if n + 1 < NTILES:
                        exps(n + 1)
                    if n < 2 * NT:
                        act.wait_ge(pT_done, n + 1)
                        act.activation(probsT[:, n % 2, 0, :], ps[:, 4, :], ACT.Copy).then_inc(pT_act, 1)
                for b in range(TR_STAT, TR_COEF, 2):
                    copy_stat(tr_copy, b)
                for g in range(NGROUP):
                    act.wait_ge(stat_step, 3 + g)
                    act.activation(stat[:, 0, g, :], stat[:, 0, g, :], ACT.Exp).then_inc(stat_exp, 1)
                copy_coef(tr_copy)
                for b in range(TR_O, TR_O + 12):
                    if b % 2 == 0:
                        copy_o(tr_copy, b)
                act.wait_ge(pool_lin, 1)
                for tt in range(2):
                    for n in range(2):
                        a = act.activation(mixT[:, tt, n * HALF:(n + 1) * HALF], ps[:, 2 * tt + n, :], ACT.Copy,
                                           scale=pool_scale[:, tt:tt + 1])
                a.then_inc(mix_pool, 1)

            def project_out():
                act.wait_ge(mix_pool, 1)
                for b in (TR_O + 10, TR_O + 11):
                    tr_copied(act, b)
                us = [(OUT_U0[hf], l, hf) for hf in (0, 1) for l in range(OUT_UNITS)]
                for n, (u0, l, hf) in enumerate(us):
                    if n == 0:
                        for a, b, c in us[0:2]:
                            split(a, 0, b, mixT[:, b, c * HALF:(c + 1) * HALF])
                    if n + 2 < len(us):
                        a, b, c = us[n + 2]
                        split(a, 0, b, mixT[:, b, c * HALF:(c + 1) * HALF])
                    else:
                        split(GU_U0[2], 0, n + 2 - len(us))
                    if l == OUT_UNITS - 1:
                        evac_y(Y_OF_MIX[hf], (y, y_b)[hf], u0 + l)

            sq2(0, JOBS[0])
            for i in range(HT):
                if i + 1 < HT:
                    sq2(i + 1, JOBS[0])
                x_hi_part(i, JOBS[0])
            split(GU_U0[0], 0, 0)
            split(GU_U0[0], 0, 1)
            gate_up(0, JOBS[1])
            down(0, GU_U0[1])
            gate_up(1, JOBS[2])
            down(1, IN_U0[0])
            project_in(0, JOBS[3])
            project_in(1, None)
            attention()
            project_out()
            act.wait_ge(zeroed, 4)
            for i in range(HT):
                sq1(i, JOBS[4])
                sq2(i, JOBS[4])
                x_hi_part(i, JOBS[4])
            gate_up(2, JOBS[5])
            down(2, GU_U0[3])
            gate_up(3, JOBS[6])
            down(3, None)
            for i in range(HT):
                sq1(i, JOBS[7])

        @block.vector
        def _(dve):
            dve.sem_inc(lo_done, LO_CREDIT)
            dve.sem_inc(h_done, H_CREDIT)

            def split(u0, t, k, src=None):
                s = (u0 + k) % SPLIT_SLOTS
                dve.wait_ge(hi_done, t * BLOCK + (u0 + k + 1))
                w = dve.tensor_tensor(w_lo[:, s, :], raw[:, (u0 + k) % RAW_SLOTS, :], w_hi[:, s, :].bitcast(F32),
                                      ALU.subtract)
                if src is not None:
                    w = dve.tensor_tensor(hs_lo[:, s, :], src, hs_hi[:, s, :].bitcast(F32), ALU.subtract)
                w.then_inc(lo_done, 1)

            def x_new(i, job):
                n = i + job["P0"]
                dve.wait_ge(z_done, n + 1)
                dve.wait_ge(x_in, n * 16 + 16)
                dve.scalar_tensor_tensor(out=x_tile[:, :], in0=job["y"][:, bass.ds(i, 1), :].rearrange("p a b -> p (a b)"),
                                         scalar=r1[:, 0:1], in1=x_tile[:, :], op0=ALU.mult, op1=ALU.add)\
                   .then_inc(xnew_done, 1)

            def x_norm(i, job):
                n = i + job["Q0"]
                dve.wait_ge(r2_done, n + 1)
                wait(dve, xT_done, n)
                if "src" in job:
                    src = x_tile[:, :]
                else:
                    src = y[:, bass.ds(i, 1), :].rearrange("p a b -> p (a b)")
                dve.scalar_tensor_tensor(out=xn[:, :], in0=src, scalar=r2[:, 0:1], in1=g_pre[:, :],
                                         op0=ALU.mult, op1=ALU.mult).then_inc(xn_done, 1)

            def x_lo_part(i, job):
                n = i + job["Q0"]
                dve.wait_ge(xhi_done, n + 1)
                for b in (0, 1):
                    at = (slice(None), slice(4 * b, 4 * b + 4), bass.ds(i * P, P))
                    a = dve.tensor_tensor(x_lo[job["half"]][at], ps[:, 4 + b, :].rearrange("p (a c) -> p a c", a=4),
                                          x_hi[job["half"]][at].bitcast(F32), ALU.subtract)
                a.then_inc(xlo_done, 1)

            def times_up(u0, t, k, f0, j_par, dst, rows=slice(0, P), bank=None):
                dve.wait_ge(used, t * BLOCK + (u0 + k + 1 + USED_CREDIT))
                dve.wait_ge(sil_done, t * 2 + (f0 + k // 2 + 1))
                dve.tensor_tensor(dst, ps[rows, 2 * j_par + 1 if bank is None else bank, :], sil[rows, j_par, :],
                                  ALU.mult).then_inc(h_done, 1)

            def gate_up(p, side):
                u0, f0 = GU_U0[p], NFT * p

                def blk(t, side):
                    for k in range(BLOCK):
                        split(u0, t, k + 2)
                        if k % 2 == 1:
                            dst = h_all[:, bass.ds(t * 2 + k // 2, 1), :].rearrange("p a b -> p (a b)")
                            times_up(u0, t, k, f0, k // 2, dst)
                        if side and k == 0 and "src" in side:
                            x_new(t, side)
                        if side and k == 1 and "Q0" in side:
                            x_norm(t, side)
                        if side and k == 2 and "Q0" in side:
                            x_lo_part(t, side)

                dve.wait_ge(g_in, G_COUNT[JOBS.index(side)])
                with dve.Fori(0, HT) as t:
                    blk(t, side)
                with dve.Fori(HT, FT // 2) as t:
                    blk(t, None)
                T = FT // 2
                split(u0, T, 2)
                split(DOWN_U0[p], 0, 0, h_all[:, 0, :])
                times_up(u0, T, 1, f0, 0, h_all[:, FT - 1, :])
                times_up(u0, T, 2, f0, 1, h_all[0:TAIL, FT, :], slice(TAIL, P), bank=2)
                split(DOWN_U0[p], 0, 1, h_all[:, 1, :])

            def evac_y(dst, last_unit):
                dve.wait_ge(used, last_unit + 1 + USED_CREDIT)
                for i in range(HT):
                    dve.tensor_copy(dst[:, i, 512:1024], ps[:, 2 * i + 1, :]).then_inc(y_dve, 1)

            def down(p, nxt):
                u0 = DOWN_U0[p]
                with dve.Fori(0, DOWN_UNITS // BLOCK) as t:
                    for k in range(BLOCK):
                        split(u0, t, k + 2, h_all[:, bass.ds(t * BLOCK + k + 2, 1), :].rearrange("p a b -> p (a b)"))
                if nxt is not None:
                    split(nxt, 0, 0)
                    split(nxt, 0, 1)
                evac_y(y, u0 + DOWN_UNITS - 1)

            def project_in(hf, side):
                u0 = IN_U0[hf]

                def blk(t, side, last=False):
                    for k in range(BLOCK):
                        if not last or k < 2:
                            split(u0, t, k + 2)
                        elif hf == 0:
                            split(IN_U0[1], 0, k - 2)
                        if side and k == 0:
                            x_new(t, side)
                        if side and k == 1:
                            x_norm(t, side)
                        if side and k == 2:
                            x_lo_part(t, side)

                with dve.Fori(0, 4) as t:
                    blk(t, side)
                blk(4, None, True)

            def tr_copy(b, dst, src):
                dve.wait_ge(tr_done, b + 1)
                dve.tensor_copy(dst, src).then_inc(tr_dve, 1)

            def attention():
                for b in range(1, 16, 2):
                    copy_v(tr_copy, b)
                dve.wait_ge(bias_in, 16)

                def maxima(n):
                    g, T = divmod(n, NT)
                    nk = P if g == 2 else 2 * P
                    kind = {0: 0 if T == 0 else 2 if T == NT - 1 else 1, 1: 3 + T % 2, 2: 5}[g]
                    dve.wait_ge(s_done, n + 1)
                    if n >= 2:
                        dve.wait_ge(pT_done, n - 1)
                    for h in range(HPG):
                        b0 = kind * HPG * 2 * P + h * nk
                        a = dve.tensor_tensor_reduce(out=probs[:, n % 2, h, 0:nk],
                                                     in0=ps[:, 2 * (n % 2) + h % 2, h // 2 * 256:h // 2 * 256 + nk],
                                                     in1=bias[:, b0:b0 + nk], scale=QK_SCALE, scalar=-3e38,
                                                     op0=ALU.add, op1=ALU.max, accum_out=m_max[:, n, h:h + 1])
                    a.then_inc(max_part, 1)
                    dve.wait_ge(max_part, n + 1)
                    dve.tensor_scalar(m_neg[:, n, :], m_max[:, n, :], -1.0, None, ALU.mult).then_inc(smax_done, 1)

                maxima(0)
                maxima(1)
                for n in range(NTILES + 1):
                    if n < NTILES:
                        dve.wait_ge(pT_done, n + 1)
                        c = 1 if n < 2 * NT else 0
                        dve.tensor_copy(probsT[:, n % 2, c, :], ps[:, 4 + c, :]).then_inc(pT_dve, 1)
                    if n + 2 < NTILES:
                        maxima(n + 2)
                    if n >= 1:
                        dve.wait_ge(pv_done, n)
                        dve.tensor_copy(o_all[:, n - 1, :], ps[:, 6 + (n - 1) % 2, 0:HPG * HEAD]).then_inc(o_done, 1)
                for b in range(TR_STAT + 1, TR_COEF, 2):
                    copy_stat(tr_copy, b)
                for b in (TR_COEF - 2, TR_COEF - 1):
                    tr_copied(dve, b)
                steps = [0]

                def step(ins):
                    steps[0] += 1
                    ins.then_inc(stat_step, 1)

                def stepped(n):
                    dve.wait_ge(stat_step, n)

                m = [stat[:, 0, g, :] for g in range(NGROUP)]
                d = [stat[:, 1, g, :] for g in range(NGROUP)]
                step(dve.tensor_tensor(m_all_max, m[0], m[1], ALU.max))
                stepped(1)
                step(dve.tensor_tensor(m_all_max, m_all_max, m[2], ALU.max))
                stepped(2)
                for g in range(NGROUP):
                    step(dve.tensor_tensor(m[g], m[g], m_all_max, ALU.subtract))
                for g in range(NGROUP):
                    dve.wait_ge(stat_exp, g + 1)
                    step(dve.tensor_tensor(d[g], d[g], m[g], ALU.mult))
                stepped(7)
                step(dve.tensor_tensor(den_sum, d[0], d[1], ALU.add))
                stepped(9)
                step(dve.tensor_tensor(den_sum, den_sum, d[2], ALU.add))
                stepped(10)
                step(dve.reciprocal(m_all_max, den_sum))
                stepped(11)
                for g in range(NGROUP):
                    def order(ap):
                        return ap if g == 0 else ap.rearrange("p (l r) -> p r l", r=DILATION[g])

                    own = d[g] if g == 0 else d[g].rearrange("p (r l) -> p r l", r=DILATION[g])
                    dve.tensor_tensor(own, order(m[g]), order(m_all_max), ALU.mult).then_inc(coef_done, 1)
                tr_copied(dve, TR_COEF)
                scale_out(dve, 0).then_inc(scaled_dve, 1)
                scale_out(dve, 2).then_inc(scaled_dve, 1)
                for b in range(TR_O, TR_O + 12):
                    if b % 2 == 1:
                        copy_o(tr_copy, b)

            def project_out():
                dve.wait_ge(mix_pool, 1)
                us = [(OUT_U0[hf], l, hf) for hf in (0, 1) for l in range(OUT_UNITS)]
                for n, (u0, l, hf) in enumerate(us):
                    if n == 0:
                        for a, b, c in us[0:2]:
                            split(a, 0, b, mixT[:, b, c * HALF:(c + 1) * HALF])
                    if n + 2 < len(us):
                        a, b, c = us[n + 2]
                        split(a, 0, b, mixT[:, b, c * HALF:(c + 1) * HALF])
                    else:
                        split(GU_U0[2], 0, n + 2 - len(us))
                    if l == OUT_UNITS - 1:
                        evac_y((y, y_b)[hf], u0 + l)

            dve.wait_ge(g_in, 16)
            for i in range(HT):
                x_norm(i, JOBS[0])
                x_lo_part(i, JOBS[0])
            split(GU_U0[0], 0, 0)
            split(GU_U0[0], 0, 1)
            gate_up(0, JOBS[1])
            down(0, GU_U0[1])
            gate_up(1, JOBS[2])
            down(1, IN_U0[0])
            project_in(0, JOBS[3])
            project_in(1, None)
            attention()
            project_out()
            dve.wait_ge(g_in, G_COUNT[4])
            for i in range(HT):
                x_new(i, JOBS[4])
                x_norm(i, JOBS[4])
                x_lo_part(i, JOBS[4])
            gate_up(2, JOBS[5])
            down(2, GU_U0[3])
            gate_up(3, JOBS[6])
            down(3, None)
            for i in range(HT):
                x_new(i, JOBS[7])

        @block.gpsimd
        def _(pool):
            pool.memset(neg_half[:, :], -0.5).then_inc(zeroed, 1)
            pool.memset(sel_w[:, :, :], 0.0).then_inc(zeroed, 1)
            pool.memset(h_all[:, FT, :], 0.0).then_inc(zeroed, 1)
            pool.wait_ge(zeroed, 3)

            def rstd(ss, ms, r, ms_done, n, half):
                f = 4.0 if half else 1.0
                pool.tensor_scalar(ms[:, :], ss[:, :], f / D, f * RMS_EPS, ALU.mult, ALU.add).then_inc(ms_done, 1)
                pool.wait_ge(ms_done, n + 1)
                return pool.tensor_tensor(r[:, :], ms[:, :], neg_half[:, :], ALU.pow)

            def tile(i, job, last=False):
                if "src" in job:
                    n = i + job["P0"]
                    row = bass.ds(i * P + job["half"] * HALF, P)
                    pool.dma_start(x_tile[:, :], job["src"][row, :]).then_inc(x_in, 16)
                    pool.wait_ge(sq1_done, n + 1)
                    rstd(ss1, ms1, r1, ms1_done, n, job["d"] not in Y_OF_MIX)
                    yt = job["y"][:, bass.ds(i, 1), :].rearrange("p a b -> p (a b)")
                    pool.tensor_tensor(yt, yt, g_post[:, :], ALU.mult).then_inc(z_done, 1)
                    pool.wait_ge(xnew_done, n + 1)
                    pool.dma_start(job["dst"][row, :], x_tile[:, :]).then_inc(x_out, 16)
                if "Q0" in job:
                    q = i + job["Q0"]
                    pool.wait_ge(sq2_done, q + 1)
                    rstd(ss2, ms2, r2, ms2_done, q, False).then_inc(r2_done, 1)
                    pool.wait_ge(xn_done, q + 1)
                if "src" in job:
                    pool.wait_ge(x_out, n * 16 + 16)

            def gains(post, pre):
                if post:
                    pool.dma_start(g_post[:, :], io[post].to_broadcast([P, D])).then_inc(g_in, 16)
                if pre:
                    pool.dma_start(g_pre[:, :], io[pre].to_broadcast([P, D])).then_inc(g_in, 16)

            def job(n):
                pool.wait_ge(g_in, G_COUNT[n])
                for i in range(HT):
                    tile(i, JOBS[n])

            def pooling():
                n = [0]

                def step(ins):
                    n[0] += 1
                    ins.then_inc(pool_step, 1)
                    pool.wait_ge(pool_step, n[0])

                pool.wait_ge(const_in, 6 * 16)
                pool.wait_ge(z_evac, 2 * IN_UNITS + Z_CREDIT)
                pool.wait_ge(s_done, NTILES)
                END = PAD + SEQ
                src, dst = win_a, win_b
                step(pool.memset(src[:, :, 0:PAD], 0.0))
                step(pool.tensor_copy(src[:, :, PAD:END], u_pool))
                for lvl, w in enumerate(POOL_WINDOWS):
                    s = w // 2
                    step(pool.tensor_tensor(dst[:, :, 0:END - s], src[:, :, 0:END - s], src[:, :, s:END], ALU.add))
                    step(pool.tensor_copy(dst[:, :, END - s:END], src[:, :, END - s:END]))
                    tt, rows = lvl // 2, slice(lvl % 2 * HEAD, (lvl % 2 + 1) * HEAD)
                    mean, u = dst[rows, tt, PAD - s:END - s], u_pool[rows, tt, :]
                    step(pool.tensor_scalar(mean, mean, 1.0 / w, None, ALU.mult))
                    step(pool.tensor_tensor(mean[:, 0:PAD], mean[:, 0:PAD], edge[rows, tt, 0:PAD], ALU.mult))
                    step(pool.tensor_tensor(mean[:, SEQ - PAD:SEQ], mean[:, SEQ - PAD:SEQ],
                                            edge[rows, tt, PAD:2 * PAD], ALU.mult))
                    step(pool.tensor_tensor(u, mean, u, ALU.subtract))
                    src, dst = dst, src
                assert n[0] == POOL_STEPS

            gains(None, "g_ffn1_pre")
            for i in range(HT):
                tile(i, JOBS[0])
            for n in (1, 2, 3):
                if n == 2:
                    gains("g_ffn1_post", "g_mix_pre")
                job(n)
            gains("g_mix_post", "g_ffn2_pre")
            pooling()
            tr_copied(pool, TR_COEF)
            scale_out(pool, 1).then_inc(scaled, 1)
            pool.memset(h_all[:, FT, :], 0.0).then_inc(zeroed, 1)
            for n in (4, 5):
                job(n)
            gains("g_ffn2_post", None)
            for n in (6, 7):
                job(n)

        @block.tensor
        def _(pe):
            pe.sem_inc(used, USED_CREDIT)

            def split_ready(u0, t, k):
                pe.wait_ge(lo_done, t * BLOCK + (u0 + k + 1 + LO_CREDIT))
                return (u0 + k) % SPLIT_SLOTS

            def weights_by_x(u0, t, k, half, bank):
                s = split_ready(u0, t, k)
                hi = w_hi[:, s, :].rearrange("p (a f) -> p a f", a=DT)
                lo = w_lo[:, s, :].rearrange("p (a f) -> p a f", a=DT)
                for a in range(DT):
                    pe.matmul(ps[:, bank, :], hi[:, a, :], x_hi[half][:, a, :], start=(a == 0), stop=False)
                    pe.matmul(ps[:, bank, :], hi[:, a, :], x_lo[half][:, a, :], start=False, stop=False)
                    mm = pe.matmul(ps[:, bank, :], lo[:, a, :], x_hi[half][:, a, :], start=False, stop=(a == DT - 1))
                mm.then_inc(used, 1)

            def transposes(i, job):
                n = i + job["Q0"]
                pe.wait_ge(xn_done, n + 1)
                wait(pe, xlo_done, n)
                for a in range(DT):
                    mm = pe.transpose(ps[:, 4 + a // 4, a % 4 * P:(a % 4 + 1) * P], xn[:, a * P:(a + 1) * P],
                                      ident[:, :])
                mm.then_inc(xT_done, 1)

            def y_banks_free(d, bank):
                if d is not None:
                    pe.wait_ge(y_act if bank % 2 == 0 else y_dve, d * HT + bank // 2 + 1)

            def gate_up(p, half, side, d):
                u0, f0 = GU_U0[p], NFT * p

                def unit(t, k, side=None):
                    if k == 3 and side and "Q0" in side:
                        y_banks_free(d, 4)
                        y_banks_free(d, 5)
                        transposes(t, side)
                    if k % 2 == 0:
                        pe.wait_ge(h_done, t * 2 + (f0 + k // 2 - 1 + H_CREDIT))
                    y_banks_free(d, k)
                    weights_by_x(u0, t, k, half, k)

                pe.wait_ge(xlo_done, side["Q0"] if "Q0" in side else 24)
                with pe.Fori(0, HT) as t:
                    for k in range(BLOCK):
                        unit(t, k, side)
                with pe.Fori(HT, FT // 2) as t:
                    for k in range(BLOCK):
                        unit(t, k)
                for k in range(3):
                    unit(FT // 2, k)

            def accumulate(u0, t, k, first, last, rows=slice(0, P), after=None):
                s = split_ready(u0, t, k)
                for i in ACC_ORDER:
                    if after is not None and i == 0:
                        pe.wait_ge(*after)
                    hi, lo = hs_hi[rows, s, i * P:(i + 1) * P], hs_lo[rows, s, i * P:(i + 1) * P]
                    for n in (0, 1):
                        acc, cols = ps[:, 2 * i + n, :], slice(n * 512, (n + 1) * 512)
                        pe.matmul(acc, hi, w_hi[rows, s, cols], start=first, stop=False)
                        pe.matmul(acc, hi, w_lo[rows, s, cols], start=False, stop=False)
                        mm = pe.matmul(acc, lo, w_hi[rows, s, cols], start=False, stop=last)
                mm.then_inc(used, 1)

            def down(p):
                u0 = DOWN_U0[p]
                for k in range(BLOCK):
                    accumulate(u0, 0, k, k == 0, False, after=(h_done, NFT * (p + 1) + H_CREDIT) if k == 0 else None)
                with pe.Fori(1, DOWN_UNITS // BLOCK) as t:
                    for k in range(BLOCK):
                        accumulate(u0, t, k, False, False)
                T = DOWN_UNITS // BLOCK
                accumulate(u0, T, 0, False, False)
                accumulate(u0, T, 1, False, True, slice(0, TAIL))

            def project_in(hf, side, d):
                u0 = IN_U0[hf]
                pe.wait_ge(xlo_done, 12 + 4 * hf)

                def blk(t, side):
                    for k in range(BLOCK):
                        if side and k == 3:
                            y_banks_free(d, 4)
                            y_banks_free(d, 5)
                            transposes(t, side)
                        y_banks_free(d, k)
                        pe.wait_ge(z_evac, t * BLOCK + (hf * IN_UNITS + k - 3 + Z_CREDIT))
                        weights_by_x(u0, t, k, hf, k)

                with pe.Fori(0, HT) as t:
                    blk(t, side)
                with pe.Fori(HT, IN_UNITS // BLOCK) as t:
                    blk(t, None)

            def tr_bank(b):
                if b >= 4:
                    tr_copied(pe, b - 4)
                return 4 + b % 4

            def attention():
                pe.wait_ge(z_evac, 2 * IN_UNITS - 2 + Z_CREDIT)
                for b in range(16):
                    bank = tr_bank(b)
                    g, c, off = (b // 4, b % 4, 0) if b < 12 else (0, b - 12, SIDE)
                    for e in range(2 if b < 15 else 1):
                        for w in range(2):
                            k0 = (2 * c + e) * P + off
                            mm = pe.transpose(ps[:, bank, (2 * e + w) * P:(2 * e + w + 1) * P],
                                              vT[:, 2 * g + w, k0:k0 + P], ident[:, :])
                    mm.then_inc(tr_done, 1)

                def window(n):
                    g, T = divmod(n, NT)
                    if g == 0:
                        if T == 0:
                            return 0, [v_nat[:, 0, 0, :], v_nat[:, 0, 1, :]]
                        if T == NT - 1:
                            return SEQ - 2 * P, [v_nat[:, 0, NT - 2, :], v_nat[:, 0, NT - 1, :]]
                        return T * P - SIDE, [v_mid[:, T - 1, :], v_mid[:, T, :]]
                    if g == 1:
                        a = T // 2 * 2
                        return a * P, [v_nat[:, 1, a, :], v_nat[:, 1, a + 1, :]]
                    return T * P, [v_nat[:, 2, T, :]]

                def scores(n):
                    g, T = divmod(n, NT)
                    k0, vs = window(n)
                    nk = len(vs) * P
                    if n >= 2:
                        pe.wait_ge(smax_done, n - 1)
                    for h in range(HPG):
                        r = slice(h % 2 * HEAD, h % 2 * HEAD + HEAD)
                        mm = pe.matmul(ps[:, 2 * (n % 2) + h % 2, h // 2 * 256:h // 2 * 256 + nk],
                                       qk[r, 2 * g + h // 2, T * P:(T + 1) * P],
                                       qk[r, 6 + 2 * g + h // 2, k0:k0 + nk], start=True, stop=True)
                    mm.then_inc(s_done, 1)

                def turn(n):
                    vs = window(n)[1]
                    pe.wait_ge(exp_done, n + 1)
                    if n >= 1:
                        pe.wait_ge(pT_dve, n)
                        pe.wait_ge(pT_act, min(n, 2 * NT))
                    for c in range(len(vs)):
                        for h in range(HPG):
                            mm = pe.transpose(ps[:, 4 + c, h * P:(h + 1) * P], probs[:, n % 2, h, c * P:(c + 1) * P],
                                              ident[:, :])
                    mm.then_inc(pT_done, 1)

                def values(n):
                    vs = window(n)[1]
                    pe.wait_ge(pT_dve, n + 1)
                    pe.wait_ge(pT_act, min(n + 1, 2 * NT))
                    if n >= 2:
                        pe.wait_ge(o_done, n - 1)
                    for h in range(HPG):
                        for c, v in enumerate(vs):
                            mm = pe.matmul(ps[:, 6 + n % 2, h * HEAD:(h + 1) * HEAD],
                                           probsT[:, n % 2, c, h * P:(h + 1) * P], v[:, h * HEAD:(h + 1) * HEAD],
                                           start=(c == 0), stop=(c == len(vs) - 1))
                    mm.then_inc(pv_done, 1)

                for b in range(12, 16):
                    tr_copied(pe, b)
                pe.wait_ge(z_evac, 2 * IN_UNITS + Z_CREDIT)
                scores(0)
                scores(1)
                for n in range(NTILES + 1):
                    if n < NTILES:
                        turn(n)
                    if n + 2 < NTILES:
                        scores(n + 2)
                    if n >= 1:
                        values(n - 1)
                pe.wait_ge(o_done, NTILES)
                for b in range(TR_STAT, TR_COEF):
                    s, g, c = (b - TR_STAT) // 6, (b - TR_STAT) % 6 // 2, b % 2
                    bank = tr_bank(b)
                    for T in range(4):
                        src = (m_max, den)[s][:, g * NT + 4 * c + T, :]
                        mm = pe.transpose(ps[0:HPG, bank, T * P:(T + 1) * P], src, ident[:, :])
                    mm.then_inc(tr_done, 1)
                pe.wait_ge(pool_step, POOL_STEPS)
                for tt in range(2):
                    for n in range(2):
                        mm = pe.matmul(ps[:, 2 * tt + n, :], sel_w[:, tt, :], u_pool[:, tt, n * HALF:(n + 1) * HALF],
                                       start=True, stop=True)
                mm.then_inc(pool_lin, 1)
                pe.wait_ge(coef_done, NGROUP)
                bank = tr_bank(TR_COEF)
                for n in range(NTILES):
                    g, T = divmod(n, NT)
                    src = stat[:, 1, g, T * P:(T + 1) * P]
                    mm = pe.transpose(ps[:, bank, n * HPG:(n + 1) * HPG], src, ident[0:HPG, 0:HPG])
                mm.then_inc(tr_done, 1)
                for b in range(TR_O, TR_O + 12):
                    g, w, c = (b - TR_O) // 4, (b - TR_O) // 2 % 2, (b - TR_O) % 2
                    if (b - TR_O) % 4 == 0:
                        if g == 1:
                            pe.wait_ge(scaled, 1)
                        else:
                            pe.wait_ge(scaled_dve, 1 + g // 2)
                    bank = tr_bank(b)
                    for T in range(4):
                        mm = pe.transpose(ps[:, bank, T * P:(T + 1) * P],
                                          o_all[:, g * NT + 4 * c + T, w * P:(w + 1) * P], ident[:, :])
                    mm.then_inc(tr_done, 1)

            def project_out():
                for b in range(TR_O + 8, TR_O + 12):
                    tr_copied(pe, b)
                for hf in (0, 1):
                    if hf == 1:
                        for bank in range(8):
                            y_banks_free(2, bank)
                    for l in range(OUT_UNITS):
                        accumulate(OUT_U0[hf], 0, l, l == 0, l == OUT_UNITS - 1)

            pe.wait_ge(ident_in, 16)
            for i in range(HT):
                transposes(i, JOBS[0])
            gate_up(0, 0, JOBS[1], None)
            down(0)
            gate_up(1, 1, JOBS[2], 0)
            down(1)
            project_in(0, JOBS[3], 1)
            project_in(1, None, 1)
            attention()
            project_out()
            for bank in (4, 5):
                y_banks_free(3, bank)
            for i in range(HT):
                transposes(i, JOBS[4])
            gate_up(2, 0, JOBS[5], 3)
            down(2)
            gate_up(3, 1, JOBS[6], 4)
            down(3)


def constants():
    slopes = np.array([2.0 ** (-8.0 * (i + 1) / N_HEADS) for i in range(N_HEADS)], np.float32)
    q, k2, k1 = np.arange(P)[:, None], np.arange(2 * P)[None, :], np.arange(P)[None, :]

    def biases(g, rel, valid):
        out = [np.where(valid, -(slopes[g * HPG + h] * (np.abs(rel) * DILATION[g]).astype(np.float32)) / QK_SCALE, MASKED)
               for h in range(HPG)]
        return [np.asarray(o, np.float32) for o in out]

    parts = []
    for g, off in ((0, 0), (0, -SIDE), (0, -P), (1, 0), (1, -P)):
        rel = off + k2 - q
        parts += biases(g, rel, np.abs(rel) <= SIDE)
    parts += biases(2, k1 - q, k1 // HEAD == q // HEAD)
    edge = np.ones((P, 2, 2 * PAD), np.float32)
    for lvl, w in enumerate(POOL_WINDOWS):
        rows, tt = slice(lvl % 2 * HEAD, (lvl % 2 + 1) * HEAD), lvl // 2
        for t in range(w // 2):
            edge[rows, tt, t] = w / (t + w // 2)
        for t in range(1, w // 2):
            edge[rows, tt, 2 * PAD - t] = w / (w // 2 + t)
    return {"ident": np.eye(P, dtype=np.float32), "bias": np.concatenate(parts, axis=1), "edge": edge}


def kernel(**inputs):
    import concourse.bacc as bacc
    from concourse.bass_utils import run_bass_kernel_spmd

    nc = bacc.Bacc("TRN2", target_bir_lowering=False, num_devices=1)
    arrays = {}
    for name, a in inputs.items():
        a = np.ascontiguousarray(a)
        if name == "x" or name.startswith("w"):
            a = a[0]
        if name == "pool_scale":
            a = np.ascontiguousarray(a.reshape(2, P).T)
        arrays[name] = a
    arrays.update(constants())
    io = {n: nc.dram_tensor(f"in_{n}_dram", a.shape, F32, kind="ExternalInput").ap() for n, a in arrays.items()}
    out = nc.dram_tensor("out_dram", (SEQ, D), F32, kind="ExternalOutput").ap()
    xs1 = nc.dram_tensor("xs1_dram", (SEQ, D), F32).ap()
    xs2 = nc.dram_tensor("xs2_dram", (SEQ, D), F32).ap()
    layer_program(nc, io, out, xs1, xs2)
    r = run_bass_kernel_spmd(nc, [{f"in_{n}_dram": a for n, a in arrays.items()}], core_ids=[0])
    return r.results[0]["out_dram"].reshape(1, SEQ, D)
```

```python
from contextlib import ExitStack

import numpy as np
import concourse.bass as bass
from concourse import mybir

F32 = mybir.dt.float32
F32R = mybir.dt.float32r
ALU = mybir.AluOpType
ACT = mybir.ActivationFunctionType
AX = mybir.AxisListType

P = 128
SEQ, D = 1024, 1024
HALF = SEQ // 2
HT = HALF // P
DT = D // P
FF = 64 * -(-8 * D // (3 * 64))
FT = FF // P
TAIL = FF - FT * P
NFT = FT + 1
HEAD = 64
NGROUP, HPG = 3, 4
POOL_DIM = D // 4
POOL_WINDOWS = (2, 4, 8, 16)
DILATION = (1, 4, 16)
N_HEADS = NGROUP * HPG
SIDE = 64
RMS_EPS = 1e-6
QK_SCALE = HEAD ** -0.5
MASKED = 1e30
NT = SEQ // P
NTILES = NGROUP * NT
PAD = max(POOL_WINDOWS) // 2
SLOPES = [float(np.float32(2.0 ** (-8.0 * (i + 1) / N_HEADS))) for i in range(N_HEADS)]
STAT_EXP = 6
POOL_STEPS = 1 + 2 * (2 + 4) + 4 * len(POOL_WINDOWS)

RAW_SLOTS, SPLIT_SLOTS = 4, 2
BLOCK = 4
GU_UNITS = 2 * FT + 1
DOWN_UNITS = NFT
IN_UNITS = (POOL_DIM + 3 * N_HEADS * HEAD) // P
OUT_UNITS = DT
OUT_TILES = [(0, 1, 2), (3, 4, 5), (6, 7)]
_sizes = [GU_UNITS, DOWN_UNITS] * 2 + [IN_UNITS] * 2 + [OUT_UNITS] * 3 + [GU_UNITS, DOWN_UNITS] * 2
_starts = [sum(_sizes[:n]) for n in range(len(_sizes) + 1)]
GU_U0 = [_starts[0], _starts[2], _starts[9], _starts[11]]
DOWN_U0 = [_starts[1], _starts[3], _starts[10], _starts[12]]
IN_U0 = [_starts[4], _starts[5]]
OUT_U0 = _starts[6]
UNITS = _starts[-1]
TAIL_UNITS = [u0 + GU_UNITS - 1 for u0 in GU_U0]
Y0_FFN = [0, 4, 16, 20]
Y0_LAST_OUT = 14
FIN0_FFN = [0, 3, 11, 14]
FIN0_OUT = [6, 8, 10]

LO_CREDIT, USED_CREDIT, H_CREDIT, Z_CREDIT = RAW_SLOTS, SPLIT_SLOTS, 2, 2

ACC_ORDER = (2, 3, 0, 1)

_groups = [2 + 6 * a + 2 * g + e for g in range(NGROUP) for a in range(3) for e in range(2)]
IN_COLS = [_groups + [0, 1], [0, 1] + _groups]

STEPS = NTILES + 3
SCHEDULE = {
    (6, "end"): [("step", 0)],
    (7, "mid"): [("step", 1)], (7, "end"): [("step", 2)],
    (8, "end"): [("v", b) for b in range(0, 4)],
    (9, "mid"): [("v", b) for b in range(4, 8)],
    (9, "end"): [("step", 3)],
    (10, "mid"): [("step", 4)], (10, "end"): [("step", 5)],
    (11, "mid"): [("step", 6)], (11, "end"): [("step", 7)],
    (12, "end"): [("step", 8)],
    (13, "mid"): [("step", 9)], (13, "end"): [("step", 10)],
    (14, "mid"): [("v", 8)], (14, "end"): [("v", 9)],
    (15, "mid"): [("v", 10)], (15, "end"): [("v", 11), ("step", 11)],
    (16, "mid"): [("step", 12)], (16, "end"): [("step", 13)],
    (17, "mid"): [("step", 14)], (17, "end"): [("step", 15)],
    (18, "end"): [("step", 16)],
    (19, "mid"): [("step", 17)], (19, "end"): [("step", 18)],
}
AFTER_IN = [("v", 12), ("v", 13), ("v", 14), ("v", 15), ("step", 19), ("step", 20), ("stat", 16), ("step", 21),
            ("stat", 17), ("step", 22), ("stat", 18), ("step", 23), ("stat", 19)]\
    + [("step", m) for m in range(24, STEPS)]

TR_STAT1, TR_STAT2, TR_NAT, TR_ROWS, TR_COEF, TR_O, TR_END = 16, 20, 24, 25, 29, 30, 42
TR_BANK = [4 + b % 4 for b in range(8)] + [7] * 4 + [7, 0, 1, 7] + [7] * 4 + [0, 1, 2, 3] + [0] + [1, 2, 3, 0] + [1]\
    + [(2, 3, 0, 1)[b % 4] for b in range(12)]
TR_ON_ACT = [b % 2 == 0 for b in range(TR_NAT)] + [False] + [True, False, True, False] + [False]\
    + [b % 2 == 0 for b in range(12)]


def s_banks(n):
    return 0 if n >= 19 and n % 2 else 2


def loaded_count(u0, t, k):
    u = u0 + k
    if isinstance(t, int):
        t, u = 0, u + BLOCK * t
    tails = sum(1 for v in TAIL_UNITS if v <= u and v % RAW_SLOTS == u % RAW_SLOTS)
    return (t + u // RAW_SLOTS + 1 + tails) * 16


def natural(ap, g, c):
    if g == 0:
        return ap[:, c * HALF:(c + 1) * HALF]
    d = DILATION[g]
    n = d // 2
    return ap.rearrange("p (l r) -> p r l", r=d)[:, c * n:(c + 1) * n, :]


def as_permuted(ap, g):
    if g == 0:
        return ap
    return ap.rearrange("p (r l) -> p r l", r=DILATION[g] // 2)


def own_half(dst, src, g, c):
    if g == 0:
        return dst[:, c * HALF:(c + 1) * HALF], src
    d = DILATION[g]
    n = HALF // d
    return (dst.rearrange("p (r l) -> p r l", r=d)[:, :, c * n:(c + 1) * n], src.rearrange("p (l r) -> p r l", r=d))


def layer_program(nc, io, out, xs1, xs2):
    ctx = ExitStack()
    with ctx:
        def sb(name, shape, dt=F32):
            return ctx.enter_context(nc.sbuf_tensor(name, shape, dt))

        def sem(name):
            return ctx.enter_context(nc.semaphore(name))

        raw = sb("raw", [P, RAW_SLOTS, D])
        w_hi = sb("w_hi", [P, SPLIT_SLOTS, D], F32R)
        w_lo = sb("w_lo", [P, SPLIT_SLOTS, D], F32R)
        with ExitStack() as first:
            y = first.enter_context(nc.sbuf_tensor("y", [P, HT, D], F32))
        with ExitStack() as second:
            u_pad = second.enter_context(nc.sbuf_tensor("u_pad", [P, 2, PAD + SEQ], F32))
            probsT = second.enter_context(nc.sbuf_tensor("probsT", [P, 2, 2, HPG * P], F32))
        sb("region_y", [P, 2 * (PAD + SEQ) + 2 * SEQ])
        with ExitStack() as first:
            x_tile = first.enter_context(nc.sbuf_tensor("x_tile", [P, D], F32))
            xn = first.enter_context(nc.sbuf_tensor("xn", [P, D], F32))
        with ExitStack() as second:
            probs = second.enter_context(nc.sbuf_tensor("probs", [P, 2, HPG, 2 * P], F32))
        sb("region_x", [P, 2 * D])
        with ExitStack() as first:
            g_post = first.enter_context(nc.sbuf_tensor("g_post", [P, D], F32))
            g_pre = first.enter_context(nc.sbuf_tensor("g_pre", [P, D], F32))
        with ExitStack() as second:
            wins = [second.enter_context(nc.sbuf_tensor(f"win{n}", [P, PAD + SEQ], F32)) for n in (0, 1)]
        sb("region_g", [P, 2 * (PAD + SEQ)])
        ident = sb("ident", [P, P])
        distance = sb("distance", [P, 3 * 2 * P + P])
        edge = sb("edge", [P, 2, 2 * PAD])
        pool_scale = sb("pool_scale", [P, 2])
        neg_half = sb("neg_half", [P, 1])
        ss1, ms1, r1, ss2, ms2, r2 = (sb(n, [P, HT]) for n in ("ss1", "ms1", "r1", "ss2", "ms2", "r2"))
        m_neg = sb("m_neg", [P, NTILES * HPG])
        den = sb("den", [P, NTILES * HPG])
        coef = sb("coef", [P, NTILES * HPG])
        nat = sb("nat", [P, 2, NGROUP, NT * HPG])
        m_all = sb("m_all", [P, NT * HPG])
        den_sum = sb("den_sum", [P, NT * HPG])

        with ExitStack() as first:
            x_hi, x_lo = [None, None], [None, None]
            for n in (0, 1):
                x_hi[n] = first.enter_context(nc.sbuf_tensor(f"x_hi{n}", [P, DT, HALF], F32R))
                x_lo[n] = first.enter_context(nc.sbuf_tensor(f"x_lo{n}", [P, DT, HALF], F32R))
        with ExitStack() as second:
            v_nat = second.enter_context(nc.sbuf_tensor("v_nat", [P, NGROUP, NT, HPG * HEAD], F32))
            v_mid = second.enter_context(nc.sbuf_tensor("v_mid", [P, NT - 1, HPG * HEAD], F32))
            sel_w = second.enter_context(nc.sbuf_tensor("sel_w", [P, 2, P], F32))
        sb("region1", [P, 2 * 2 * DT * HALF])

        with ExitStack() as first:
            h_all = first.enter_context(nc.sbuf_tensor("h_all", [P, NFT, HALF], F32))
            hs_hi = first.enter_context(nc.sbuf_tensor("hs_hi", [P, SPLIT_SLOTS, HALF], F32R))
            hs_lo = first.enter_context(nc.sbuf_tensor("hs_lo", [P, SPLIT_SLOTS, HALF], F32R))
            sil = first.enter_context(nc.sbuf_tensor("sil", [P, 2, HALF], F32))
            y_b = first.enter_context(nc.sbuf_tensor("y_b", [P, HT, D], F32))
        with ExitStack() as second:
            qk = second.enter_context(nc.sbuf_tensor("qk", [P, 12, SEQ], F32))
            vT = second.enter_context(nc.sbuf_tensor("vT", [P, 6, SEQ], F32))
        with ExitStack() as third:
            mixT = third.enter_context(nc.sbuf_tensor("mixT", [P, DT, SEQ], F32))
            rows_ = third.enter_context(nc.sbuf_tensor("rows_", [HPG, 2, 2, SEQ], F32))
        sb("region2", [P, 18 * SEQ])
        o_all = vT[:, :, :].rearrange("p t (n e) -> p (t n) e", e=HPG * HEAD)
        junk_sb = sil[:, :, :].rearrange("p a b -> p (a b)")

        ps = ctx.enter_context(nc.psum_tensor("ps", [P, 8, 512], F32))
        junk = ps[:, 6:8, :].rearrange("p a b -> p (a b)")

        w_loaded = [sem(f"w_loaded{n}") for n in range(RAW_SLOTS)]
        hi_done = sem("hi_done")
        lo_done = sem("lo_done")
        used = sem("used")
        sil_done = sem("sil_done")
        h_done = sem("h_done")
        y_act = sem("y_act")
        y_dve = sem("y_dve")
        ident_in = sem("ident_in")
        const_in = sem("const_in")
        w_pool_in = sem("w_pool_in")
        x_last_in = sem("x_last_in")
        y_fin = sem("y_fin")
        g_in = sem("g_in")
        y_in = [sem(f"y_in{n}") for n in range(HT)]
        y_half1_in = sem("y_half1_in")
        sq1_done = sem("sq1_done")
        ms1_done = sem("ms1_done")
        last_scaled = sem("last_scaled")
        last_dve = sem("last_dve")
        last_pool = sem("last_pool")
        last_out = sem("last_out")
        z_done = sem("z_done")
        x_in = sem("x_in")
        xnew_done = sem("xnew_done")
        x_out = sem("x_out")
        sq2_done = sem("sq2_done")
        ms2_done = sem("ms2_done")
        r2_done = sem("r2_done")
        xn_done = sem("xn_done")
        xT_done = sem("xT_done")
        xhi_done = sem("xhi_done")
        xlo_done = sem("xlo_done")
        z_evac = sem("z_evac")
        tr_done = sem("tr_done")
        tr_act = sem("tr_act")
        tr_dve = sem("tr_dve")
        s_done = sem("s_done")
        biased = sem("biased")
        smax_done = sem("smax_done")
        exp_done = sem("exp_done")
        pT_done = sem("pT_done")
        pT_act = sem("pT_act")
        pT_dve = sem("pT_dve")
        pv_done = sem("pv_done")
        o_done = sem("o_done")
        stat_step = sem("stat_step")
        stat_exp = sem("stat_exp")
        coef_done = sem("coef_done")
        scaled = sem("scaled")
        scaled_dve = sem("scaled_dve")
        pool_step = sem("pool_step")
        pool_lin = sem("pool_lin")
        mix_pool = sem("mix_pool")
        zeroed = sem("zeroed")

        def wait(eng, s, n):
            if not isinstance(n, int) or n > 0:
                eng.wait_ge(s, n)

        x_in_dram = io["x"]
        JOBS = [
            dict(half=0, y=y, Q0=0), dict(half=1, y=y, Q0=4),
            dict(half=0, y=y, src=x_in_dram, dst=xs1, y0=0, need=4, P0=0, Q0=8),
            dict(half=1, y=y, src=x_in_dram, dst=xs1, y0=4, need=8, P0=4, Q0=12),
            dict(half=0, y=y, src=xs1, dst=xs2, y0=8, P0=8, Q0=16),
            dict(half=1, y=y_b, src=xs1, dst=xs2, y0=12, need=16, P0=12, Q0=20),
            dict(half=0, y=y, src=xs2, dst=out, y0=16, need=20, P0=16),
        ]
        G_COUNT = [16, 16, 48, 48, 80, 80, 96]
        OUT_SIDE = {8: 0, 11: 1, 14: 2, 17: 3}

        def tr_copied(eng, b):
            on_act = TR_ON_ACT[b]
            eng.wait_ge(tr_act if on_act else tr_dve, sum(1 for a in TR_ON_ACT[:b + 1] if a == on_act))

        def copy_v(copy, b):
            bank = ps[:, TR_BANK[b], :]
            if 4 <= b < 8:
                c = b - 4
                n = 2 if c < 3 else 1
                copy(b, v_mid[:, 2 * c:2 * c + n, :].rearrange("p a b -> p (a b)"), bank[:, 0:n * HPG * HEAD])
            else:
                g, c = (0, b) if b < 4 else ((b - 4) // 4, b % 4)
                copy(b, v_nat[:, g, 2 * c:2 * c + 2, :].rearrange("p a b -> p (a b)"), bank)

        def copy_stat(copy, b):
            g, s, c = 1 + (b - TR_STAT1) // 4, b // 2 % 2, b % 2
            copy(b, natural(rows_[:, g - 1, s, :], g, c), as_permuted(ps[0:HPG, TR_BANK[b], :], g))

        def copy_coef_rows(copy, b):
            g, c = 1 + (b - TR_ROWS) // 2, (b - TR_ROWS) % 2
            copy(b, *own_half(rows_[:, g - 1, 0, :], ps[0:HPG, TR_BANK[b], :], g, c))

        def copy_o(copy, b):
            g, w, c = (b - TR_O) // 4, (b - TR_O) // 2 % 2, (b - TR_O) % 2
            copy(b, natural(mixT[:, 2 + 2 * g + w, :], g, c), as_permuted(ps[:, TR_BANK[b], :], g))

        def x_parts(i, job, bank):
            return [((slice(None), slice(4 * b, 4 * b + 4), bass.ds(i * P, P)),
                     ps[:, bank + b, :].rearrange("p (a c) -> p a c", a=4)) for b in (0, 1)]

        def mix_y(i):
            return (y, y_b)[i // HT][:, i % HT, :]

        def scale_out(eng, g):
            o = o_all[:, g * NT:(g + 1) * NT, :].rearrange("p n (h e) -> p (n h) e", e=HEAD)
            c = coef[:, g * NT * HPG:(g + 1) * NT * HPG].rearrange("p (a o) -> p a o", o=1)
            return eng.tensor_tensor(o, o, c.to_broadcast([P, NT * HPG, HEAD]), ALU.mult)

        block = ctx.enter_context(nc.Block())

        @block.sync
        def _(sp):
            def load(u0, t, k, dst_cols, src):
                sp.wait_ge(lo_done, t * BLOCK + (u0 + k - RAW_SLOTS + 1 + LO_CREDIT))
                slot = (u0 + k) % RAW_SLOTS
                for cols, s in zip(dst_cols, src):
                    sp.dma_start(cols(raw[:, slot, :]), s).then_inc(w_loaded[slot], 16)

            def columns(w, start, n=P):
                return w.rearrange("(a p) f -> p a f", p=P)[:, :, bass.ds(start, n)]

            def col_tile(ap):
                return ap.rearrange("p (a f) -> p a f", a=DT)

            def gate_up(p, u0):
                gate, up = io[f"w{p}_gate"], io[f"w{p}_up"]

                def tile(t, k):
                    load(u0, t, k, [col_tile], [columns((gate, up)[k % 2], t * 2 * P + k // 2 * P)])

                first = 1 if u0 == 0 else 0
                if first:
                    for k in range(BLOCK):
                        tile(0, k)
                    small_and_second_half()
                with sp.Fori(first, FT // 2) as t:
                    for k in range(BLOCK):
                        tile(t, k)
                for k in range(2):
                    tile(FT // 2, k)
                load(u0, FT // 2, 2, [lambda ap: col_tile(ap)[:, :, 0:TAIL], lambda ap: col_tile(ap)[:, :, TAIL:P]],
                     [columns(gate, FT * P, TAIL), columns(up, FT * P, TAIL)])

            def rows(w, u0, n, tail):
                def tile(t, k, count=P):
                    load(u0, t, k, [lambda ap: ap[0:count, :]], [w[bass.ds(t * BLOCK * P + k * P, count), :]])

                with sp.Fori(0, n // BLOCK) as t:
                    for k in range(BLOCK):
                        tile(t, k)
                for k in range(n % BLOCK):
                    tile(n // BLOCK, k, tail if k == n % BLOCK - 1 else P)

            for i in range(HT):
                sp.dma_start(y[:, i, :], io["x"][i * P:(i + 1) * P, :]).then_inc(y_in[i], 16)
                if i == 0:
                    sp.dma_start(ident[:, :], io["ident"]).then_inc(ident_in, 16)

            def small_and_second_half():
                for ap, name in ((edge[:, :, :], "edge"), (pool_scale[:, :], "pool_scale"),
                                 (distance[:, :], "distance")):
                    sp.dma_start(ap, io[name]).then_inc(const_in, 16)
                sp.wait_ge(xn_done, HT)
                sp.dma_start(y[:, :, :], io["x"][HALF:SEQ, :].rearrange("(i p) d -> p i d", p=P))\
                  .then_inc(y_half1_in, 16)

            for p in (0, 1):
                gate_up(1, GU_U0[p])
                rows(io["w1_down"], DOWN_U0[p], DOWN_UNITS, TAIL)
            for hf in (0, 1):
                for l, col in enumerate(IN_COLS[hf]):
                    load(IN_U0[hf], 0, l, [col_tile], [columns(io["w_in"], col * P)])
            for n in range(len(OUT_TILES)):
                rows(io["w_out"], OUT_U0 + n * OUT_UNITS, OUT_UNITS, P)
            for p in (2, 3):
                gate_up(2, GU_U0[p])
                rows(io["w2_down"], DOWN_U0[p], DOWN_UNITS, TAIL)
            for i in range(HT):
                sp.wait_ge(*((last_pool, 1) if i == 1 else (last_dve, (1, 0, 2, 3)[i])))
                sp.dma_start(out[HALF + i * P:HALF + (i + 1) * P, :], y[:, i, :]).then_inc(last_out, 16)
            sp.wait_ge(last_out, 16 * HT)

        @block.scalar
        def _(act):
            act.sem_inc(z_evac, Z_CREDIT)

            def split(u0, t, k, src=None, ready=None):
                s = (u0 + k) % SPLIT_SLOTS
                act.wait_ge(w_loaded[(u0 + k) % RAW_SLOTS], loaded_count(u0, t, k))
                act.wait_ge(used, t * BLOCK + (u0 + k - SPLIT_SLOTS + 1 + USED_CREDIT))
                w = act.activation(w_hi[:, s, :], raw[:, (u0 + k) % RAW_SLOTS, :], ACT.Copy)
                if src is not None:
                    if ready is not None:
                        act.wait_ge(*ready)
                    w = act.activation(hs_hi[:, s, 0:src.shape[-1]], src, ACT.Copy)
                w.then_inc(hi_done, 1)

            def sq1(i, job, junk=junk):
                if "need" in job:
                    act.wait_ge(y_act, job["need"])
                    act.wait_ge(y_dve, job["need"])
                else:
                    act.wait_ge(y_act, job["y0"] + i + 1)
                    act.wait_ge(y_dve, job["y0"] + i + 1)
                if "Q0" not in job:
                    act.wait_ge(z_done, i + job["P0"])
                act.activation(junk, job["y"][:, bass.ds(i, 1), :].rearrange("p a b -> p (a b)"), ACT.Square,
                               accum_out=ss1[:, 0:1]).then_inc(sq1_done, 1)

            def sq2(i, job, junk=junk, c=0):
                if c == 0:
                    wait(act, ms2_done, i + job["Q0"])
                if "src" in job:
                    act.wait_ge(xnew_done, i + job["P0"] + 1)
                    src = x_tile[:, :]
                else:
                    act.wait_ge(y_in[i] if job["half"] == 0 else y_half1_in, 16)
                    src = y[:, bass.ds(i, 1), :].rearrange("p a b -> p (a b)")
                act.activation(junk, src, ACT.Square, accum_out=ss2[:, c:c + 1]).then_inc(sq2_done, 1)

            def x_hi_part(i, job, bank=4):
                act.wait_ge(xT_done, i + job["Q0"] + 1)
                for at, src in x_parts(i, job, bank):
                    a = act.activation(x_hi[job["half"]][at], src, ACT.Copy)
                a.then_inc(xhi_done, 1)

            def silu(u0, t, k, f0, j_par, rows_in=slice(0, P), rows_out=slice(0, P)):
                act.wait_ge(used, t * BLOCK + (u0 + k + 1 + USED_CREDIT))
                act.wait_ge(h_done, t * 2 + (f0 + k // 2 - 1 + H_CREDIT))
                act.activation(sil[rows_out, j_par, :], ps[rows_in, 2 * j_par, :], ACT.Silu).then_inc(sil_done, 1)

            def gate_up(p, side=None):
                u0, f0 = GU_U0[p], NFT * p

                def blk(t, side):
                    for k in range(BLOCK):
                        split(u0, t, k + 2)
                        if side and k == 0 and "src" in side:
                            sq1(t, side)
                        if side and k == 1 and "Q0" in side:
                            sq2(t, side)
                        if k % 2 == 0:
                            silu(u0, t, k, f0, k // 2)
                        if side and k == 2 and "Q0" in side:
                            x_hi_part(t, side)

                with act.Fori(0, HT) as t:
                    blk(t, side)
                with act.Fori(HT, FT // 2) as t:
                    blk(t, None)
                T = FT // 2
                split(u0, T, 2)
                silu(u0, T, 0, f0, 0)
                split(DOWN_U0[p], 0, 0, h_all[:, 0, :], (h_done, f0 + 1 + H_CREDIT))
                silu(u0, T, 2, f0, 1, slice(0, TAIL), slice(TAIL, P))
                split(DOWN_U0[p], 0, 1, h_all[:, 1, :], (h_done, f0 + 2 + H_CREDIT))

            def evac_y(y0, fin0, dst, tiles, last_unit):
                for q, i in enumerate(tiles):
                    if q < len(tiles) - 1:
                        act.wait_ge(y_fin, fin0 + q + 1)
                    else:
                        act.wait_ge(used, last_unit + 1 + USED_CREDIT)
                    act.activation(dst[q], ps[:, 2 * q, :], ACT.Copy).then_inc(y_act, 1)

            def down(p, nxt):
                u0, f0 = DOWN_U0[p], NFT * p

                def sp2(t, k):
                    src = h_all[:, bass.ds(t * BLOCK + k + 2, 1), :].rearrange("p a b -> p (a b)")
                    split(u0, t, k + 2, src, (h_done, t * BLOCK + (f0 + k + 3 + H_CREDIT)))

                with act.Fori(0, DOWN_UNITS // BLOCK) as t:
                    for k in range(BLOCK):
                        sp2(t, k)
                if nxt is not None:
                    split(nxt, 0, 0)
                    split(nxt, 0, 1)
                    evac_y(Y0_FFN[p], FIN0_FFN[p], [y[:, i, 0:512] for i in range(HT)], range(HT), u0 + DOWN_UNITS - 1)

            def project_in(hf, side):
                u0 = IN_U0[hf]
                for l in range(IN_UNITS):
                    t, k = l // BLOCK, l % BLOCK
                    if hf == 1:
                        items(SCHEDULE.get((l, "mid"), []))
                    if l + 2 < IN_UNITS:
                        split(u0, 0, l + 2)
                    elif hf == 0:
                        split(IN_U0[1], 0, l + 2 - IN_UNITS)
                    if side and t < HT:
                        if k == 0:
                            sq1(t, side)
                        if k == 1:
                            sq2(t, side)
                        if k == 2:
                            x_hi_part(t, side)
                    act.wait_ge(used, u0 + l + 1 + USED_CREDIT)
                    src, scale = ps[:, l % 2, :], 1.0
                    col = IN_COLS[hf][l]
                    if col < 2:
                        if l == IN_UNITS - 2:
                            act.wait_ge(sq1_done, 2 * HT)
                            act.wait_ge(xnew_done, 2 * HT)
                        dst = u_pad[:, col, PAD + hf * HALF:PAD + (hf + 1) * HALF]
                    else:
                        g, a, e = (col - 2) // 2 % 3, (col - 2) // 6, col % 2
                        if a == 0:
                            scale = QK_SCALE
                        dst = vT[:, 2 * g + e, :] if a == 2 else qk[:, 6 * a + 2 * g + e, :]
                        dst, src = own_half(dst, src, g, hf)
                    act.activation(dst, src, ACT.Copy, scale=scale).then_inc(z_evac, 1)
                    if hf == 1:
                        items(SCHEDULE.get((l, "end"), []))

            def tr_copy(b, dst, src):
                act.wait_ge(tr_done, b + 1)
                act.activation(dst, src, ACT.Copy).then_inc(tr_act, 1)

            def exps(n):
                act.wait_ge(smax_done, n + 1)
                nk = P if n >= 2 * NT else 2 * P
                for h in range(HPG):
                    a = act.activation(probs[:, n % 2, h, 0:nk], probs[:, n % 2, h, 0:nk], ACT.Exp,
                                       bias=m_neg[:, n * HPG + h:n * HPG + h + 1],
                                       accum_out=den[:, n * HPG + h:n * HPG + h + 1])
                a.then_inc(exp_done, 1)

            def items(todo):
                for what, n in todo:
                    if what == "step":
                        if 0 <= n - 2 < 2 * NT:
                            act.wait_ge(pT_done, n - 1)
                            act.activation(probsT[:, n % 2, 0, :], ps[:, 4, :], ACT.Copy).then_inc(pT_act, 1)
                        if n < NTILES:
                            exps(n)
                    elif TR_ON_ACT[n]:
                        (copy_v if what == "v" else copy_stat)(tr_copy, n)

            def joint_softmax():
                for b in range(TR_STAT2, TR_NAT):
                    if TR_ON_ACT[b]:
                        copy_stat(tr_copy, b)
                act.wait_ge(pool_lin, 1)
                for tt in range(2):
                    for n in range(2):
                        a = act.activation(mixT[:, tt, n * HALF:(n + 1) * HALF], ps[:, 4 + 2 * tt + n, :], ACT.Copy,
                                           scale=pool_scale[:, tt:tt + 1])
                a.then_inc(mix_pool, 1)
                act.wait_ge(stat_step, STAT_EXP)
                e = nat[:, 0, :, :].rearrange("p g n -> p (g n)")
                act.activation(e, e, ACT.Exp).then_inc(stat_exp, 1)
                for b in range(TR_ROWS, TR_COEF):
                    if TR_ON_ACT[b]:
                        copy_coef_rows(tr_copy, b)
                for b in range(TR_O, TR_END):
                    if TR_ON_ACT[b]:
                        copy_o(tr_copy, b)

            def out_split(n):
                if n < 3 * OUT_UNITS:
                    tiles = OUT_TILES[n // OUT_UNITS]
                    split(OUT_U0, 0, n, mixT[:, n % OUT_UNITS, tiles[0] * P:(tiles[-1] + 1) * P])
                else:
                    split(OUT_U0, 0, n)

            def project_out():
                tr_copied(act, TR_END - 2)
                tr_copied(act, TR_END - 1)
                out_split(0)
                out_split(1)
                for n in range(3 * OUT_UNITS):
                    out_split(n + 2)
                    for base, i in OUT_SIDE.items():
                        if n == base:
                            sq1(i, JOBS[4], junk_sb)
                        if n == base + 1:
                            sq2(i, JOBS[4], junk_sb)
                        if n == base + 3:
                            x_hi_part(i, JOBS[4], 6)
                    p = n // OUT_UNITS
                    if n % OUT_UNITS == OUT_UNITS - 1:
                        evac_y(8 + 3 * p, FIN0_OUT[p], [mix_y(i)[:, 0:512] for i in OUT_TILES[p]], OUT_TILES[p],
                               OUT_U0 + n)

            def last_tiles():
                for i in range(HT):
                    if i < HT - 1:
                        act.wait_ge(y_fin, FIN0_FFN[3] + i + 1)
                    else:
                        act.wait_ge(used, UNITS + USED_CREDIT)
                    if i >= 2:
                        act.wait_ge(sq1_done, JOBS[6]["P0"] + HT + i - 1)
                    act.activation((g_pre, xn)[i % 2][:, :], ps[:, 2 * i:2 * i + 2, :].rearrange("p a b -> p (a b)"),
                                   ACT.Square, accum_out=ss1[:, i:i + 1]).then_inc(sq1_done, 1)

            for i in range(HT):
                bank = i % 2 * 2
                if i >= 2:
                    act.wait_ge(sq2_done, i - 1)
                sq2(i, JOBS[0], ps[:, bank:bank + 2, :].rearrange("p a b -> p (a b)"), i)
            x_hi_part(0, JOBS[0], 4)
            split(GU_U0[0], 0, 0)
            x_hi_part(1, JOBS[0], 6)
            x_hi_part(2, JOBS[0], 4)
            split(GU_U0[0], 0, 1)
            x_hi_part(3, JOBS[0], 6)
            act.wait_ge(xlo_done, HT)
            gate_up(0, JOBS[1])
            down(0, GU_U0[1])
            gate_up(1, JOBS[2])
            down(1, IN_U0[0])
            project_in(0, JOBS[3])
            project_in(1, None)
            items(AFTER_IN)
            joint_softmax()
            project_out()
            act.wait_ge(zeroed, 5)
            act.wait_ge(xlo_done, JOBS[5]["Q0"])
            gate_up(2, JOBS[5])
            down(2, GU_U0[3])
            gate_up(3, JOBS[6])
            down(3, None)
            last_tiles()

        @block.vector
        def _(dve):
            dve.sem_inc(lo_done, LO_CREDIT)
            dve.sem_inc(h_done, H_CREDIT)

            def split(u0, t, k, src=None):
                s = (u0 + k) % SPLIT_SLOTS
                dve.wait_ge(hi_done, t * BLOCK + (u0 + k + 1))
                w = dve.tensor_tensor(w_lo[:, s, :], raw[:, (u0 + k) % RAW_SLOTS, :], w_hi[:, s, :].bitcast(F32),
                                      ALU.subtract)
                if src is not None:
                    n = src.shape[-1]
                    w = dve.tensor_tensor(hs_lo[:, s, 0:n], src, hs_hi[:, s, 0:n].bitcast(F32), ALU.subtract)
                w.then_inc(lo_done, 1)

            def x_new(i, job):
                n = i + job["P0"]
                dve.wait_ge(z_done, n + 1)
                dve.wait_ge(x_in, n * 16 + 16)
                dve.scalar_tensor_tensor(out=x_tile[:, :], in0=job["y"][:, bass.ds(i, 1), :].rearrange("p a b -> p (a b)"),
                                         scalar=r1[:, 0:1], in1=x_tile[:, :], op0=ALU.mult, op1=ALU.add)\
                   .then_inc(xnew_done, 1)

            def x_norm(i, job, dst=xn, c=0):
                n = i + job["Q0"]
                dve.wait_ge(r2_done, n + 1)
                if dst is xn:
                    dve.wait_ge(xT_done, n)
                if "src" in job:
                    src = x_tile[:, :]
                else:
                    src = y[:, bass.ds(i, 1), :].rearrange("p a b -> p (a b)")
                dve.scalar_tensor_tensor(out=dst[:, :], in0=src, scalar=r2[:, c:c + 1], in1=g_pre[:, :],
                                         op0=ALU.mult, op1=ALU.mult).then_inc(xn_done, 1)

            def x_lo_part(i, job, bank=4):
                dve.wait_ge(xhi_done, i + job["Q0"] + 1)
                for at, src in x_parts(i, job, bank):
                    a = dve.tensor_tensor(x_lo[job["half"]][at], src, x_hi[job["half"]][at].bitcast(F32), ALU.subtract)
                a.then_inc(xlo_done, 1)

            def times_up(u0, t, k, f0, j_par, dst, rows=slice(0, P), bank=None):
                dve.wait_ge(used, t * BLOCK + (u0 + k + 1 + USED_CREDIT))
                dve.wait_ge(sil_done, t * 2 + (f0 + k // 2 + 1))
                dve.tensor_tensor(dst, ps[rows, 2 * j_par + 1 if bank is None else bank, :], sil[rows, j_par, :],
                                  ALU.mult).then_inc(h_done, 1)

            def gate_up(p, side):
                u0, f0 = GU_U0[p], NFT * p

                def blk(t, side):
                    for k in range(BLOCK):
                        split(u0, t, k + 2)
                        if k % 2 == 1:
                            dst = h_all[:, bass.ds(t * 2 + k // 2, 1), :].rearrange("p a b -> p (a b)")
                            times_up(u0, t, k, f0, k // 2, dst)
                        if side and k == 0 and "src" in side:
                            x_new(t, side)
                        if side and k == 1 and "Q0" in side:
                            x_norm(t, side)
                        if side and k == 2 and "Q0" in side:
                            x_lo_part(t, side)

                dve.wait_ge(g_in, G_COUNT[JOBS.index(side)])
                with dve.Fori(0, HT) as t:
                    blk(t, side)
                with dve.Fori(HT, FT // 2) as t:
                    blk(t, None)
                T = FT // 2
                split(u0, T, 2)
                split(DOWN_U0[p], 0, 0, h_all[:, 0, :])
                times_up(u0, T, 1, f0, 0, h_all[:, FT - 1, :])
                times_up(u0, T, 2, f0, 1, h_all[0:TAIL, FT, :], slice(TAIL, P), bank=2)
                split(DOWN_U0[p], 0, 1, h_all[:, 1, :])

            def evac_y(fin0, dst, last_unit):
                for q, at in enumerate(dst):
                    if q < len(dst) - 1:
                        dve.wait_ge(y_fin, fin0 + q + 1)
                    else:
                        dve.wait_ge(used, last_unit + 1 + USED_CREDIT)
                    dve.tensor_copy(at, ps[:, 2 * q + 1, :]).then_inc(y_dve, 1)

            def down(p, nxt):
                u0 = DOWN_U0[p]
                with dve.Fori(0, DOWN_UNITS // BLOCK) as t:
                    for k in range(BLOCK):
                        split(u0, t, k + 2, h_all[:, bass.ds(t * BLOCK + k + 2, 1), :].rearrange("p a b -> p (a b)"))
                if nxt is not None:
                    split(nxt, 0, 0)
                    split(nxt, 0, 1)
                    evac_y(FIN0_FFN[p], [y[:, i, 512:1024] for i in range(HT)], u0 + DOWN_UNITS - 1)

            def project_in(hf, side):
                u0 = IN_U0[hf]

                def blk(t, side, last=False):
                    for k in range(BLOCK):
                        if not last or k < 2:
                            split(u0, t, k + 2)
                        else:
                            split(IN_U0[1], 0, k - 2)
                        if side and k == 0:
                            x_new(t, side)
                        if side and k == 1:
                            x_norm(t, side)
                        if side and k == 2:
                            x_lo_part(t, side)

                if hf == 0:
                    with dve.Fori(0, 4) as t:
                        blk(t, side)
                    blk(4, None, True)
                else:
                    dve.wait_ge(x_out, 16 * 2 * HT)
                    dve.wait_ge(const_in, 3 * 16)
                    for l in range(IN_UNITS):
                        items(SCHEDULE.get((l, "mid"), []))
                        if l + 2 < IN_UNITS:
                            split(u0, 0, l + 2)
                        items(SCHEDULE.get((l, "end"), []))

            def tr_copy(b, dst, src):
                dve.wait_ge(tr_done, b + 1)
                dve.tensor_copy(dst, src).then_inc(tr_dve, 1)

            def maxima(n):
                g, T = divmod(n, NT)
                nk = P if g == 2 else 2 * P
                d0 = {0: 0 if T == 0 else 2 if T == NT - 1 else 1, 1: T % 2 * 2, 2: 3}[g] * 2 * P
                dve.wait_ge(s_done, n + 1)
                for h in range(HPG):
                    a = dve.scalar_tensor_tensor(out=probs[:, n % 2, h, 0:nk], in0=distance[:, d0:d0 + nk],
                                                 scalar=-SLOPES[g * HPG + h] * DILATION[g],
                                                 in1=ps[:, s_banks(n) + h % 2, h // 2 * 256:h // 2 * 256 + nk],
                                                 op0=ALU.mult, op1=ALU.add)
                a.then_inc(biased, 1)
                dve.wait_ge(biased, n + 1)
                dve.tensor_reduce(m_neg[:, n * HPG:(n + 1) * HPG], probs[:, n % 2, :, 0:nk], AX.X, ALU.max,
                                  negate=True).then_inc(smax_done, 1)

            def items(todo):
                for what, n in todo:
                    if what == "step":
                        if 0 <= n - 2 < NTILES:
                            dve.wait_ge(pT_done, n - 1)
                            c = 1 if n - 2 < 2 * NT else 0
                            dve.tensor_copy(probsT[:, n % 2, c, :], ps[:, 4 + c, :]).then_inc(pT_dve, 1)
                        if n < NTILES:
                            maxima(n)
                        if 0 <= n - 3 < NTILES:
                            dve.wait_ge(pv_done, n - 2)
                            dve.tensor_copy(o_all[:, n - 3, :], ps[:, 6, 0:HPG * HEAD]).then_inc(o_done, 1)
                    elif not TR_ON_ACT[n]:
                        (copy_v if what == "v" else copy_stat)(tr_copy, n)

            def joint_softmax():
                for b in range(TR_STAT2, TR_NAT):
                    if not TR_ON_ACT[b]:
                        copy_stat(tr_copy, b)
                steps = [0]

                def step(ins):
                    steps[0] += 1
                    ins.then_inc(stat_step, 1)

                def all_steps():
                    dve.wait_ge(stat_step, steps[0])

                step(dve.tensor_copy(nat[:, 0, 0, :], m_neg[:, 0:NT * HPG]))
                dve.wait_ge(exp_done, NT)
                step(dve.tensor_copy(nat[:, 1, 0, :], den[:, 0:NT * HPG]))
                dve.wait_ge(tr_done, TR_NAT + 1)
                back = ps[:, TR_BANK[TR_NAT], 0:4 * NT * HPG].rearrange("p (g s n) -> p g s n", g=2, s=2)
                for t in (0, 1):
                    a = dve.tensor_copy(nat[:, t, 1:3, :], back[:, :, t, :])
                    step(a) if t == 0 else a.then_inc(tr_dve, 1)
                tr_copied(dve, TR_NAT)
                all_steps()
                step(dve.tensor_tensor(m_all[:, :], nat[:, 0, 0, :], nat[:, 0, 1, :], ALU.min))
                all_steps()
                step(dve.tensor_tensor(m_all[:, :], m_all[:, :], nat[:, 0, 2, :], ALU.min))
                all_steps()

                def each(ap):
                    return ap.rearrange("p (o n) -> p o n", o=1).to_broadcast([P, NGROUP, NT * HPG])

                step(dve.tensor_tensor(nat[:, 0, :, :], each(m_all[:, :]), nat[:, 0, :, :], ALU.subtract))
                assert steps[0] == STAT_EXP
                dve.wait_ge(stat_exp, 1)
                step(dve.tensor_tensor(nat[:, 1, :, :], nat[:, 1, :, :], nat[:, 0, :, :], ALU.mult))
                all_steps()
                step(dve.tensor_tensor(den_sum[:, :], nat[:, 1, 0, :], nat[:, 1, 1, :], ALU.add))
                all_steps()
                step(dve.tensor_tensor(den_sum[:, :], den_sum[:, :], nat[:, 1, 2, :], ALU.add))
                all_steps()
                step(dve.reciprocal(m_all[:, :], den_sum[:, :]))
                all_steps()
                dve.tensor_tensor(nat[:, 0, :, :], nat[:, 0, :, :], each(m_all[:, :]), ALU.mult).then_inc(coef_done, 1)
                dve.wait_ge(coef_done, 1)
                dve.tensor_copy(coef[:, 0:NT * HPG], nat[:, 0, 0, :]).then_inc(coef_done, 1)
                for b in range(TR_ROWS, TR_COEF):
                    if not TR_ON_ACT[b]:
                        copy_coef_rows(tr_copy, b)
                tr_copy(TR_COEF, coef[:, NT * HPG:], ps[:, TR_BANK[TR_COEF], 0:2 * NT * HPG])
                tr_copied(dve, TR_COEF)
                scale_out(dve, 1).then_inc(scaled_dve, 1)
                scale_out(dve, 2).then_inc(scaled_dve, 1)
                for b in range(TR_O, TR_END):
                    if not TR_ON_ACT[b]:
                        copy_o(tr_copy, b)

            def out_split(n):
                if n < 3 * OUT_UNITS:
                    tiles = OUT_TILES[n // OUT_UNITS]
                    split(OUT_U0, 0, n, mixT[:, n % OUT_UNITS, tiles[0] * P:(tiles[-1] + 1) * P])
                else:
                    split(OUT_U0, 0, n)

            def project_out():
                out_split(0)
                out_split(1)
                dve.wait_ge(g_in, G_COUNT[4])
                for n in range(3 * OUT_UNITS):
                    out_split(n + 2)
                    for base, i in OUT_SIDE.items():
                        if n == base:
                            x_new(i, JOBS[4])
                        if n == base + 1:
                            x_norm(i, JOBS[4])
                        if n == base + 3:
                            x_lo_part(i, JOBS[4], 6)
                    p = n // OUT_UNITS
                    if n % OUT_UNITS == OUT_UNITS - 1:
                        evac_y(FIN0_OUT[p], [mix_y(i)[:, 512:1024] for i in OUT_TILES[p]], OUT_U0 + n)

            def last_tiles():
                dve.wait_ge(x_last_in, 16)
                for i in range(HT):
                    dve.wait_ge(z_done, JOBS[6]["P0"] + HT + i + 1)
                    dve.scalar_tensor_tensor(out=y[:, i, :], in0=ps[:, 2 * i:2 * i + 2, :].rearrange("p a b -> p (a b)"),
                                             scalar=r1[:, i:i + 1], in1=g_post[:, :], op0=ALU.mult, op1=ALU.mult)\
                       .then_inc(last_scaled, 1)
                    if i != 1:
                        dve.wait_ge(last_scaled, i + 1)
                        dve.tensor_tensor(y[:, i, :], y[:, i, :], y_b[:, i, :], ALU.add).then_inc(last_dve, 1)

            dve.wait_ge(g_in, 16)
            first = JOBS[0]
            x_norm(0, first, y_b[:, 0, :], 0)
            x_norm(1, first, y_b[:, 1, :], 1)
            x_lo_part(0, first, 4)
            x_norm(2, first, y_b[:, 2, :], 2)
            split(GU_U0[0], 0, 0)
            x_lo_part(1, first, 6)
            x_norm(3, first, y_b[:, 3, :], 3)
            x_lo_part(2, first, 4)
            split(GU_U0[0], 0, 1)
            x_lo_part(3, first, 6)
            gate_up(0, JOBS[1])
            down(0, GU_U0[1])
            gate_up(1, JOBS[2])
            down(1, IN_U0[0])
            project_in(0, JOBS[3])
            project_in(1, None)
            items(AFTER_IN)
            joint_softmax()
            project_out()
            gate_up(2, JOBS[5])
            down(2, GU_U0[3])
            gate_up(3, JOBS[6])
            down(3, None)
            last_tiles()

        @block.gpsimd
        def _(pool):
            pool.memset(neg_half[:, :], -0.5).then_inc(zeroed, 1)
            pool.memset(h_all[:, FT, :], 0.0).then_inc(zeroed, 1)
            pool.wait_ge(zeroed, 2)

            def rstd(ss, ms, r, ms_done, n, half, c=0):
                f = 4.0 if half else 1.0
                c = slice(c, c + 1)
                pool.tensor_scalar(ms[:, c], ss[:, c], f / D, f * RMS_EPS, ALU.mult, ALU.add).then_inc(ms_done, 1)
                pool.wait_ge(ms_done, n + 1)
                return pool.tensor_tensor(r[:, c], ms[:, c], neg_half[:, :], ALU.pow)

            def tile(i, job):
                if "src" in job:
                    n = i + job["P0"]
                    row = bass.ds(i * P + job["half"] * HALF, P)
                    pool.dma_start(x_tile[:, :], job["src"][row, :]).then_inc(x_in, 16)
                    pool.wait_ge(sq1_done, n + 1)
                    rstd(ss1, ms1, r1, ms1_done, n, job["y0"] in Y0_FFN)
                    yt = job["y"][:, i, :]
                    pool.tensor_tensor(yt, yt, g_post[:, :], ALU.mult).then_inc(z_done, 1)
                    pool.wait_ge(xnew_done, n + 1)
                    pool.dma_start(job["dst"][row, :], x_tile[:, :]).then_inc(x_out, 16)
                if "Q0" in job:
                    q = i + job["Q0"]
                    pool.wait_ge(sq2_done, q + 1)
                    rstd(ss2, ms2, r2, ms2_done, q, False).then_inc(r2_done, 1)
                    pool.wait_ge(xn_done, q + 1)
                if "src" in job:
                    pool.wait_ge(x_out, n * 16 + 16)

            def gains(post, pre):
                if post:
                    pool.dma_start(g_post[:, :], io[post].to_broadcast([P, D])).then_inc(g_in, 16)
                if pre:
                    pool.dma_start(g_pre[:, :], io[pre].to_broadcast([P, D])).then_inc(g_in, 16)

            def job(n):
                pool.wait_ge(g_in, G_COUNT[n])
                for i in range(HT):
                    tile(i, JOBS[n])

            def pooling():
                n = [0]

                def step(ins):
                    n[0] += 1
                    ins.then_inc(pool_step, 1)
                    pool.wait_ge(pool_step, n[0])

                pool.wait_ge(z_evac, IN_UNITS + 2 + Z_CREDIT)
                END = PAD + SEQ
                step(pool.memset(u_pad[:, :, 0:PAD], 0.0))
                for tt in range(2):
                    src, dst = u_pad[:, tt, :], wins[0][:, :]
                    for lvl in range(2 * tt + 2):
                        w = POOL_WINDOWS[lvl]
                        s = w // 2
                        step(pool.tensor_tensor(dst[:, 0:END - s], src[:, 0:END - s], src[:, s:END], ALU.add))
                        step(pool.tensor_copy(dst[:, END - s:END], src[:, END - s:END]))
                        if lvl >= 2 * tt:
                            rows = slice(lvl % 2 * HEAD, (lvl % 2 + 1) * HEAD)
                            mean, u = dst[rows, PAD - s:END - s], u_pad[rows, tt, PAD:END]
                            step(pool.tensor_scalar(mean, mean, 1.0 / w, None, ALU.mult))
                            step(pool.tensor_tensor(mean[:, 0:PAD], mean[:, 0:PAD], edge[rows, tt, 0:PAD], ALU.mult))
                            step(pool.tensor_tensor(mean[:, SEQ - PAD:SEQ], mean[:, SEQ - PAD:SEQ],
                                                    edge[rows, tt, PAD:2 * PAD], ALU.mult))
                            step(pool.tensor_tensor(u, mean, u, ALU.subtract))
                        src, dst = dst, wins[(lvl + 1) % 2][:, :]
                assert n[0] == POOL_STEPS

            def pool_weights():
                pool.wait_ge(used, IN_U0[1] + USED_CREDIT)
                pool.memset(sel_w[:, :, :], 0.0).then_inc(zeroed, 1)
                pool.wait_ge(zeroed, 3)
                for n in range(len(POOL_WINDOWS)):
                    a = (n % 2) * HEAD
                    pool.dma_start(sel_w[a:a + HEAD, n // 2, a:a + HEAD], io["w_pool_lin"][n]).then_inc(w_pool_in, 16)

            gains(None, "g_ffn1_pre")
            for i in range(HT):
                pool.wait_ge(sq2_done, i + 1)
                rstd(ss2, ms2, r2, ms2_done, i, False, i).then_inc(r2_done, 1)
            pool.wait_ge(xn_done, HT)
            for n in (1, 2, 3):
                if n == 2:
                    gains("g_ffn1_post", "g_mix_pre")
                job(n)
            pool_weights()
            pool.wait_ge(const_in, 3 * 16)
            pooling()
            gains("g_mix_post", "g_ffn2_pre")
            pool.wait_ge(coef_done, 2)
            scale_out(pool, 0).then_inc(scaled, 1)
            tr_copied(pool, TR_COEF)
            pool.memset(h_all[:, FT, :], 0.0).then_inc(zeroed, 1)
            pool.wait_ge(zeroed, 4)
            pool.memset(neg_half[:, :], -0.5).then_inc(zeroed, 1)
            pool.wait_ge(zeroed, 5)
            for n in (4, 5):
                job(n)
            gains("g_ffn2_post", None)
            pool.dma_start(y_b[:, :, :], xs2[HALF:SEQ, :].rearrange("(i p) d -> p i d", p=P)).then_inc(x_last_in, 16)
            job(6)
            for i in range(HT):
                n = JOBS[6]["P0"] + HT + i
                pool.wait_ge(sq1_done, n + 1)
                rstd(ss1, ms1, r1, ms1_done, n, True, i).then_inc(z_done, 1)
                if i == 2:
                    pool.wait_ge(x_last_in, 16)
                    pool.wait_ge(last_scaled, 2)
                    pool.tensor_tensor(y[:, 1, :], y[:, 1, :], y_b[:, 1, :], ALU.add).then_inc(last_pool, 1)

        @block.tensor
        def _(pe):
            pe.sem_inc(used, USED_CREDIT)

            def split_ready(u0, t, k):
                pe.wait_ge(lo_done, t * BLOCK + (u0 + k + 1 + LO_CREDIT))
                return (u0 + k) % SPLIT_SLOTS

            def weights_by_x(u0, t, k, half, bank, mid=()):
                s = split_ready(u0, t, k)
                hi = w_hi[:, s, :].rearrange("p (a f) -> p a f", a=DT)
                lo = w_lo[:, s, :].rearrange("p (a f) -> p a f", a=DT)
                for a in range(DT):
                    if a == DT // 2:
                        items(mid)
                    pe.matmul(ps[:, bank, :], hi[:, a, :], x_hi[half][:, a, :], start=(a == 0), stop=False)
                    pe.matmul(ps[:, bank, :], hi[:, a, :], x_lo[half][:, a, :], start=False, stop=False)
                    mm = pe.matmul(ps[:, bank, :], lo[:, a, :], x_hi[half][:, a, :], start=False, stop=(a == DT - 1))
                mm.then_inc(used, 1)

            def transposes(i, job, bank=4, src=xn, earlier=1):
                n = i + job["Q0"]
                pe.wait_ge(xn_done, n + 1)
                wait(pe, xlo_done, n + 1 - earlier)
                for a in range(DT):
                    mm = pe.transpose(ps[:, bank + a // 4, a % 4 * P:(a % 4 + 1) * P], src[:, a * P:(a + 1) * P],
                                      ident[:, :])
                mm.then_inc(xT_done, 1)

            def y_banks_free(y0, bank):
                if y0 is not None:
                    pe.wait_ge(y_act if bank % 2 == 0 else y_dve, y0 + bank // 2 + 1)

            def gate_up(p, half, side, d):
                u0, f0 = GU_U0[p], NFT * p

                def unit(t, k, side=None):
                    if k == 3 and side and "Q0" in side:
                        if d is not None and d != Y0_LAST_OUT:
                            y_banks_free(d, 4)
                            y_banks_free(d, 5)
                        transposes(t, side)
                    if k % 2 == 0:
                        pe.wait_ge(h_done, t * 2 + (f0 + k // 2 - 1 + H_CREDIT))
                    y_banks_free(d, k)
                    weights_by_x(u0, t, k, half, k)

                pe.wait_ge(xlo_done, side["Q0"] if "Q0" in side else 24)
                with pe.Fori(0, HT) as t:
                    for k in range(BLOCK):
                        unit(t, k, side)
                with pe.Fori(HT, FT // 2) as t:
                    for k in range(BLOCK):
                        unit(t, k)
                for k in range(3):
                    unit(FT // 2, k)

            def accumulate(u0, t, k, first, last, tiles=ACC_ORDER, rows=slice(0, P), after=None):
                s = split_ready(u0, t, k)
                tiles = sorted(tiles) if last else tiles
                for i in tiles:
                    if after is not None:
                        after(i)
                    hi, lo = hs_hi[rows, s, i * P:(i + 1) * P], hs_lo[rows, s, i * P:(i + 1) * P]
                    for n in (0, 1):
                        acc, cols = ps[:, 2 * i + n, :], slice(n * 512, (n + 1) * 512)
                        pe.matmul(acc, hi, w_hi[rows, s, cols], start=first, stop=False)
                        pe.matmul(acc, hi, w_lo[rows, s, cols], start=False, stop=False)
                        mm = pe.matmul(acc, lo, w_hi[rows, s, cols], start=False, stop=last)
                    if last and i != tiles[-1]:
                        mm.then_inc(y_fin, 1)
                mm.then_inc(used, 1)

            def down(p):
                u0 = DOWN_U0[p]

                def left(i):
                    if i == 0:
                        pe.wait_ge(h_done, NFT * (p + 1) + H_CREDIT)

                for k in range(BLOCK):
                    accumulate(u0, 0, k, k == 0, False, after=left if k == 0 else None)
                with pe.Fori(1, DOWN_UNITS // BLOCK) as t:
                    for k in range(BLOCK):
                        accumulate(u0, t, k, False, False)
                T = DOWN_UNITS // BLOCK
                accumulate(u0, T, 0, False, False)
                accumulate(u0, T, 1, False, True, rows=slice(0, TAIL))

            def project_in(side, d):
                pe.wait_ge(xlo_done, side["Q0"])

                def blk(t, side):
                    for k in range(BLOCK):
                        if side and k == 3:
                            y_banks_free(d, 4)
                            y_banks_free(d, 5)
                            transposes(t, side)
                        y_banks_free(d, k % 2)
                        pe.wait_ge(z_evac, t * BLOCK + (k - 1 + Z_CREDIT))
                        weights_by_x(IN_U0[0], t, k, 0, k % 2)

                with pe.Fori(0, HT) as t:
                    blk(t, side)
                with pe.Fori(HT, IN_UNITS // BLOCK) as t:
                    blk(t, None)

            def project_in_and_attend():
                pe.wait_ge(xlo_done, 16)
                for l in range(IN_UNITS):
                    pe.wait_ge(z_evac, IN_UNITS + l - 1 + Z_CREDIT)
                    weights_by_x(IN_U0[1], 0, l, 1, l % 2, SCHEDULE.get((l, "mid"), []))
                    items(SCHEDULE.get((l, "end"), []))
                items(AFTER_IN)

            def tr_bank(b):
                before = [a for a in range(b) if TR_BANK[a] == TR_BANK[b]]
                if before:
                    tr_copied(pe, before[-1])
                return TR_BANK[b]

            def turn_v(b):
                if b < 4:
                    g, c, off, last = 0, b, 0, 8
                elif b < 8:
                    g, c, off, last = 0, b - 4, SIDE, 8
                else:
                    g, c, off, last = (b - 4) // 4, b % 4, 0, 8 + 6 * ((b - 4) // 4)
                pe.wait_ge(z_evac, IN_UNITS + last + Z_CREDIT)
                if b < 2:
                    pe.wait_ge(pT_dve, 1)
                    pe.wait_ge(pT_act, 1)
                if b in (13, 14):
                    pe.wait_ge(z_evac, 2 * IN_UNITS + Z_CREDIT)
                bank = tr_bank(b)
                for e in range(1 if b == 7 else 2):
                    for w in range(2):
                        k0 = (2 * c + e) * P + off
                        mm = pe.transpose(ps[:, bank, (2 * e + w) * P:(2 * e + w + 1) * P],
                                          vT[:, 2 * g + w, k0:k0 + P], ident[:, :])
                mm.then_inc(tr_done, 1)

            def window(n):
                g, T = divmod(n, NT)
                if g == 0:
                    if T == 0:
                        return 0, [v_nat[:, 0, 0, :], v_nat[:, 0, 1, :]]
                    if T == NT - 1:
                        return SEQ - 2 * P, [v_nat[:, 0, NT - 2, :], v_nat[:, 0, NT - 1, :]]
                    return T * P - SIDE, [v_mid[:, T - 1, :], v_mid[:, T, :]]
                if g == 1:
                    a = T // 2 * 2
                    return a * P, [v_nat[:, 1, a, :], v_nat[:, 1, a + 1, :]]
                return T * P, [v_nat[:, 2, T, :]]

            def scores(n):
                g, T = divmod(n, NT)
                k0, vs = window(n)
                nk = len(vs) * P
                pe.wait_ge(z_evac, IN_UNITS + 6 + 6 * g + Z_CREDIT)
                if n == 19:
                    tr_copied(pe, 13)
                    tr_copied(pe, 14)
                wait(pe, smax_done, n if n <= 19 else n - 1)
                for h in range(HPG):
                    r = slice(h % 2 * HEAD, h % 2 * HEAD + HEAD)
                    mm = pe.matmul(ps[:, s_banks(n) + h % 2, h // 2 * 256:h // 2 * 256 + nk],
                                   qk[r, 2 * g + h // 2, T * P:(T + 1) * P],
                                   qk[r, 6 + 2 * g + h // 2, k0:k0 + nk], start=True, stop=True)
                mm.then_inc(s_done, 1)

            def turn(n):
                vs = window(n)[1]
                pe.wait_ge(exp_done, n + 1)
                if n >= 1:
                    pe.wait_ge(pT_dve, n)
                    pe.wait_ge(pT_act, min(n, 2 * NT))
                else:
                    pe.wait_ge(xlo_done, 16)
                if n == 1:
                    tr_copied(pe, 4)
                    tr_copied(pe, 5)
                for c in range(len(vs)):
                    for h in range(HPG):
                        mm = pe.transpose(ps[:, 4 + c, h * P:(h + 1) * P], probs[:, n % 2, h, c * P:(c + 1) * P],
                                          ident[:, :])
                mm.then_inc(pT_done, 1)

            def values(n):
                vs = window(n)[1]
                pe.wait_ge(pT_dve, n + 1)
                pe.wait_ge(pT_act, min(n + 1, 2 * NT))
                tr_copied(pe, (7, 11, 15)[n // NT])
                tr_copied(pe, (6, 10, 14)[n // NT])
                if n >= 1:
                    pe.wait_ge(o_done, n)
                for h in range(HPG):
                    for c, v in enumerate(vs):
                        o = h * HEAD
                        mm = pe.matmul(ps[:, 6, o:o + HEAD], probsT[:, n % 2, c, h * P:(h + 1) * P],
                                       v[:, h * HEAD:(h + 1) * HEAD], start=(c == 0), stop=(c == len(vs) - 1))
                mm.then_inc(pv_done, 1)

            def turn_stat(b):
                g, s, c = 1 + (b - TR_STAT1) // 4, b // 2 % 2, b % 2
                pe.wait_ge(exp_done, (g + 1) * NT)
                if b >= TR_STAT2:
                    pe.wait_ge(o_done, NTILES)
                bank = tr_bank(b)
                for T in range(4):
                    n = (g * NT + 4 * c + T) * HPG
                    mm = pe.transpose(ps[0:HPG, bank, T * P:(T + 1) * P], (m_neg, den)[s][:, n:n + HPG], ident[:, :])
                mm.then_inc(tr_done, 1)

            def items(todo):
                for what, n in todo:
                    if what == "v":
                        turn_v(n)
                    elif what == "stat":
                        turn_stat(n)
                    else:
                        if 0 <= n - 2 < NTILES:
                            turn(n - 2)
                        if 0 <= n - 3 < NTILES:
                            values(n - 3)
                        if n < NTILES:
                            scores(n)

            def joint_softmax():
                for b in range(TR_STAT2, TR_NAT):
                    turn_stat(b)
                pe.wait_ge(pool_step, POOL_STEPS)
                pe.wait_ge(w_pool_in, 16 * len(POOL_WINDOWS))
                tr_copied(pe, 18)
                tr_copied(pe, 19)
                for tt in range(2):
                    for n in range(2):
                        mm = pe.matmul(ps[:, 4 + 2 * tt + n, :], sel_w[:, tt, :],
                                       u_pad[:, tt, PAD + n * HALF:PAD + (n + 1) * HALF], start=True, stop=True)
                mm.then_inc(pool_lin, 1)
                for b in range(TR_STAT2, TR_NAT):
                    tr_copied(pe, b)
                bank = tr_bank(TR_NAT)
                for g in range(2):
                    for s in range(2):
                        for j in range(NT):
                            n = ((g * 2 + s) * NT + j) * HPG
                            mm = pe.transpose(ps[:, bank, n:n + HPG], rows_[:, g, s, j * P:(j + 1) * P],
                                              ident[0:HPG, 0:HPG])
                mm.then_inc(tr_done, 1)
                pe.wait_ge(coef_done, 1)
                for b in range(TR_ROWS, TR_COEF):
                    g, c = 1 + (b - TR_ROWS) // 2, (b - TR_ROWS) % 2
                    bank = tr_bank(b)
                    for j in range(4):
                        n = (4 * c + j) * HPG
                        mm = pe.transpose(ps[0:HPG, bank, j * P:(j + 1) * P], nat[:, 0, g, n:n + HPG], ident[:, :])
                    mm.then_inc(tr_done, 1)
                for b in range(TR_ROWS, TR_COEF):
                    tr_copied(pe, b)
                bank = tr_bank(TR_COEF)
                for g in range(2):
                    for T in range(NT):
                        n = (g * NT + T) * HPG
                        mm = pe.transpose(ps[:, bank, n:n + HPG], rows_[:, g, 0, T * P:(T + 1) * P],
                                          ident[0:HPG, 0:HPG])
                mm.then_inc(tr_done, 1)
                for b in range(TR_O, TR_END):
                    g, w, c = (b - TR_O) // 4, (b - TR_O) // 2 % 2, (b - TR_O) % 2
                    if (b - TR_O) % 4 == 0:
                        if g == 0:
                            pe.wait_ge(scaled, 1)
                        else:
                            pe.wait_ge(scaled_dve, g)
                    bank = tr_bank(b)
                    for T in range(4):
                        mm = pe.transpose(ps[:, bank, T * P:(T + 1) * P],
                                          o_all[:, g * NT + 4 * c + T, w * P:(w + 1) * P], ident[:, :])
                    mm.then_inc(tr_done, 1)

            def project_out():
                for b in range(TR_END - 4, TR_END):
                    tr_copied(pe, b)
                for n in range(3 * OUT_UNITS):
                    p, l = n // OUT_UNITS, n % OUT_UNITS
                    for base, i in OUT_SIDE.items():
                        if n == base + 3:
                            transposes(i, JOBS[4], 6)

                    def left(i):
                        if p > 0:
                            y_banks_free(8 + 3 * (p - 1), 2 * i)
                            y_banks_free(8 + 3 * (p - 1), 2 * i + 1)

                    accumulate(OUT_U0, 0, n, l == 0, l == OUT_UNITS - 1, range(len(OUT_TILES[p])),
                               after=left if l == 0 else None)

            pe.wait_ge(ident_in, 16)
            for i in range(HT):
                transposes(i, JOBS[0], 4 + i % 2 * 2, y_b[:, i, :], earlier=2)
            gate_up(0, 0, JOBS[1], None)
            down(0)
            gate_up(1, 1, JOBS[2], Y0_FFN[0])
            down(1)
            project_in(JOBS[3], Y0_FFN[1])
            project_in_and_attend()
            joint_softmax()
            project_out()
            gate_up(2, 0, JOBS[5], Y0_LAST_OUT)
            down(2)
            gate_up(3, 1, JOBS[6], Y0_FFN[2])
            down(3)


def constants():
    q, k2, k1 = np.arange(P)[:, None], np.arange(2 * P)[None, :], np.arange(P)[None, :]
    parts = []
    for off in (0, -SIDE, -P):
        rel = np.abs(off + k2 - q)
        parts.append(np.where(rel <= SIDE, rel, MASKED))
    parts.append(np.where(k1 // HEAD == q // HEAD, np.abs(k1 - q), MASKED))
    edge = np.ones((P, 2, 2 * PAD), np.float32)
    for lvl, w in enumerate(POOL_WINDOWS):
        rows, tt = slice(lvl % 2 * HEAD, (lvl % 2 + 1) * HEAD), lvl // 2
        for t in range(w // 2):
            edge[rows, tt, t] = w / (t + w // 2)
        for t in range(1, w // 2):
            edge[rows, tt, 2 * PAD - t] = w / (w // 2 + t)
    return {"ident": np.eye(P, dtype=np.float32), "distance": np.concatenate(parts, axis=1).astype(np.float32),
            "edge": edge}


def kernel(**inputs):
    import concourse.bacc as bacc
    from concourse.bass_utils import run_bass_kernel_spmd

    nc = bacc.Bacc("TRN2", target_bir_lowering=False, num_devices=1)
    arrays = {}
    for name, a in inputs.items():
        a = np.ascontiguousarray(a)
        if name == "x" or name.startswith("w"):
            a = a[0]
        if name == "pool_scale":
            a = np.ascontiguousarray(a.reshape(2, P).T)
        arrays[name] = a
    arrays.update(constants())
    io = {n: nc.dram_tensor(f"in_{n}_dram", a.shape, F32, kind="ExternalInput").ap() for n, a in arrays.items()}
    out = nc.dram_tensor("out_dram", (SEQ, D), F32, kind="ExternalOutput").ap()
    xs1 = nc.dram_tensor("xs1_dram", (SEQ, D), F32).ap()
    xs2 = nc.dram_tensor("xs2_dram", (SEQ, D), F32).ap()
    layer_program(nc, io, out, xs1, xs2)
    r = run_bass_kernel_spmd(nc, [{f"in_{n}_dram": a for n, a in arrays.items()}], core_ids=[0])
    return r.results[0]["out_dram"].reshape(1, SEQ, D)
```

```python
from contextlib import ExitStack

import numpy as np
import concourse.bass as bass
from concourse import mybir

F32 = mybir.dt.float32
F32R = mybir.dt.float32r
ALU = mybir.AluOpType
ACT = mybir.ActivationFunctionType
AX = mybir.AxisListType

P = 128
SEQ, D = 1024, 1024
HALF = SEQ // 2
HT = HALF // P
DT = D // P
FF = 64 * -(-8 * D // (3 * 64))
FT = FF // P
TAIL = FF - FT * P
NFT = FT + 1
assert TAIL == P // 2
HEAD = 64
NGROUP, HPG = 3, 4
POOL_DIM = D // 4
POOL_WINDOWS = (2, 4, 8, 16)
DILATION = (1, 4, 16)
N_HEADS = NGROUP * HPG
SIDE = 64
RMS_EPS = 1e-6
QK_SCALE = HEAD ** -0.5
MASKED = 1e30
NT = SEQ // P
NTILES = NGROUP * NT
PAD = max(POOL_WINDOWS) // 2
SLOPES = [float(np.float32(2.0 ** (-8.0 * (i + 1) / N_HEADS))) for i in range(N_HEADS)]
STAT_EXP = 6
POOL_STEPS = 1 + 2 * (2 + 4) + 4 * len(POOL_WINDOWS)

RAW_SLOTS, SPLIT_SLOTS = 4, 2
BLOCK = 4
GU_UNITS = 2 * FT + 1
DOWN_UNITS = NFT
IN_UNITS = (POOL_DIM + 3 * N_HEADS * HEAD) // P
OUT_UNITS = DT
OUT_TILES = [(0, 1, 2), (3, 4, 5), (6, 7)]
_sizes = [GU_UNITS, DOWN_UNITS] * 2 + [IN_UNITS] * 2 + [OUT_UNITS] * 3 + [GU_UNITS, DOWN_UNITS] * 2
_starts = [sum(_sizes[:n]) for n in range(len(_sizes) + 1)]
GU_U0 = [_starts[0], _starts[2], _starts[9], _starts[11]]
DOWN_U0 = [_starts[1], _starts[3], _starts[10], _starts[12]]
IN_U0 = [_starts[4], _starts[5]]
OUT_U0 = _starts[6]
UNITS = _starts[-1]
TAIL_UNITS = [u0 + GU_UNITS - 1 for u0 in GU_U0] + [u0 + DOWN_UNITS - 1 for u0 in DOWN_U0]
Y0_FFN = [0, 4, 16, 20]
Y0_LAST_OUT = 14
FIN0_FFN = [0, 3, 11, 14]
FIN0_OUT = [6, 8, 10]

LO_CREDIT, USED_CREDIT, H_CREDIT, Z_CREDIT = RAW_SLOTS, SPLIT_SLOTS, 2, 2

ACC_ORDER = (2, 3, 0, 1)

_groups = [2 + 6 * a + 2 * g + e for g in range(NGROUP) for a in range(3) for e in range(2)]
IN_COLS = [_groups + [0, 1], [0, 1] + _groups]

STEPS = NTILES + 3
SCHEDULE = {
    (6, "mid"): [("step", 0)],
    (7, "mid"): [("step", 1)], (7, "end"): [("step", 2)],
    (8, "end"): [("v", b) for b in range(0, 4)],
    (9, "mid"): [("v", b) for b in range(4, 8)],
    (9, "end"): [("step", 3)],
    (10, "mid"): [("step", 4)], (10, "end"): [("step", 5)],
    (11, "mid"): [("step", 6)], (11, "end"): [("step", 7)],
    (12, "end"): [("step", 8)],
    (13, "mid"): [("step", 9)], (13, "end"): [("step", 10)],
    (14, "mid"): [("v", 8)], (14, "end"): [("v", 9)],
    (15, "mid"): [("v", 10)], (15, "end"): [("v", 11)],
    (16, "mid"): [("step", 11)], (16, "end"): [("step", 12)],
    (17, "mid"): [("step", 13)], (17, "end"): [("step", 14)],
    (18, "mid"): [("step", 15)], (18, "end"): [("step", 16)],
    (19, "mid"): [("step", 17)], (19, "end"): [("step", 18)],
}
AFTER_IN = [("v", 12), ("v", 13), ("step", 19), ("v", 14), ("step", 20), ("v", 15), ("stat", 16), ("step", 21),
            ("stat", 17), ("stat", 18), ("step", 22), ("stat", 19), ("pool", 20), ("pool", 21),
            ("step", 23), ("pool", 22), ("pool", 23), ("step", 24), ("stat", 24), ("stat", 25), ("stat", 26), ("stat", 27),
            ("step", 25), ("nat", 28), ("out", 0), ("step", 26)]

OUT_EARLY = OUT_UNITS - 1

TR_STAT1, TR_POOL, TR_STAT2, TR_NAT, TR_ROWS, TR_COEF, TR_O, TR_END = 16, 20, 24, 28, 29, 33, 34, 46
TR_BANK = [4 + b % 4 for b in range(8)] + [7] * 4 + [7, 5] * 2 + [7, 5] * 4 + [0, 1, 2, 3] + [7] + [6, 7, 6, 7] + [6]\
    + [7, 6] * 6
TR_ON_ACT = [b % 2 == 0 and b != 12 for b in range(TR_POOL)] + [True] * 4 + [b % 2 == 0 for b in range(TR_STAT2, TR_NAT)]\
    + [False] + [True, False, True, False] + [False] + [b % 2 == 0 for b in range(TR_O, TR_END)]


def s_banks(n):
    return 0 if n >= 19 and n % 2 else 2


def loaded_count(u0, t, k):
    u = u0 + k
    if isinstance(t, int):
        t, u = 0, u + BLOCK * t
    tails = sum(1 for v in TAIL_UNITS if v <= u and v % RAW_SLOTS == u % RAW_SLOTS)
    return (t + u // RAW_SLOTS + 1 + tails) * 16


def natural(ap, g, c):
    if g == 0:
        return ap[:, c * HALF:(c + 1) * HALF]
    d = DILATION[g]
    n = d // 2
    return ap.rearrange("p (l r) -> p r l", r=d)[:, c * n:(c + 1) * n, :]


def as_permuted(ap, g):
    if g == 0:
        return ap
    return ap.rearrange("p (r l) -> p r l", r=DILATION[g] // 2)


def own_half(dst, src, g, c):
    if g == 0:
        return dst[:, c * HALF:(c + 1) * HALF], src
    d = DILATION[g]
    n = HALF // d
    return (dst.rearrange("p (r l) -> p r l", r=d)[:, :, c * n:(c + 1) * n], src.rearrange("p (l r) -> p r l", r=d))


def layer_program(nc, io, out, xs1, xs2):
    ctx = ExitStack()
    with ctx:
        def sb(name, shape, dt=F32):
            return ctx.enter_context(nc.sbuf_tensor(name, shape, dt))

        def sem(name):
            return ctx.enter_context(nc.semaphore(name))

        raw = sb("raw", [P, RAW_SLOTS, D])
        w_hi = sb("w_hi", [P, SPLIT_SLOTS, D], F32R)
        w_lo = sb("w_lo", [P, SPLIT_SLOTS, D], F32R)
        with ExitStack() as first:
            y = first.enter_context(nc.sbuf_tensor("y", [P, HT, D], F32))
        with ExitStack() as second:
            u_pad = second.enter_context(nc.sbuf_tensor("u_pad", [P, 2, PAD + SEQ], F32))
            probsT = second.enter_context(nc.sbuf_tensor("probsT", [P, 2, 2, HPG * P], F32))
        sb("region_y", [P, 2 * (PAD + SEQ) + 2 * SEQ])
        with ExitStack() as first:
            x_tile = first.enter_context(nc.sbuf_tensor("x_tile", [P, D], F32))
            xn = first.enter_context(nc.sbuf_tensor("xn", [P, D], F32))
        with ExitStack() as second:
            probs = second.enter_context(nc.sbuf_tensor("probs", [P, 2, HPG, 2 * P], F32))
        sb("region_x", [P, 2 * D])
        with ExitStack() as first:
            g_post = first.enter_context(nc.sbuf_tensor("g_post", [P, D], F32))
            g_pre = first.enter_context(nc.sbuf_tensor("g_pre", [P, D], F32))
        with ExitStack() as second:
            wins = [second.enter_context(nc.sbuf_tensor(f"win{n}", [P, PAD + SEQ], F32)) for n in (0, 1)]
        with ExitStack() as third:
            q_even = third.enter_context(nc.sbuf_tensor("q_even", [P, 2, SEQ], F32))
        sb("region_g", [P, 2 * (PAD + SEQ)])
        ident = sb("ident", [P, P])
        distance = sb("distance", [P, 3 * 2 * P + P])
        edge = sb("edge", [P, 2, 2 * PAD])
        pool_scale = sb("pool_scale", [P, 2])
        neg_half = sb("neg_half", [P, 1])
        ss1, ms1, r1, ss2, ms2, r2 = (sb(n, [P, HT]) for n in ("ss1", "ms1", "r1", "ss2", "ms2", "r2"))
        m_neg = sb("m_neg", [P, NTILES * HPG])
        den = sb("den", [P, NTILES * HPG])
        coef = sb("coef", [P, NTILES * HPG])
        nat = sb("nat", [P, 2, NGROUP, NT * HPG])
        m_all = sb("m_all", [P, NT * HPG])
        den_sum = sb("den_sum", [P, NT * HPG])

        with ExitStack() as first:
            x_hi, x_lo = [None, None], [None, None]
            for n in (0, 1):
                x_hi[n] = first.enter_context(nc.sbuf_tensor(f"x_hi{n}", [P, DT, HALF], F32R))
                x_lo[n] = first.enter_context(nc.sbuf_tensor(f"x_lo{n}", [P, DT, HALF], F32R))
        with ExitStack() as second:
            v_nat = second.enter_context(nc.sbuf_tensor("v_nat", [P, NGROUP, NT, HPG * HEAD], F32))
            v_mid = second.enter_context(nc.sbuf_tensor("v_mid", [P, NT - 1, HPG * HEAD], F32))
            sel_w = second.enter_context(nc.sbuf_tensor("sel_w", [P, 2, P], F32))
            x_rows = second.enter_context(nc.sbuf_tensor("x_rows", [P, HT, D], F32))
            xn_out = second.enter_context(nc.sbuf_tensor("xn_out", [P, D], F32))
            hs_out = [second.enter_context(nc.sbuf_tensor(n, [P, SPLIT_SLOTS, 3 * P], F32R))
                      for n in ("mix_hi", "mix_lo")]
        sb("region1", [P, 2 * 2 * DT * HALF])

        with ExitStack() as first:
            h_all = first.enter_context(nc.sbuf_tensor("h_all", [P, NFT, HALF], F32))
            hs_hi = first.enter_context(nc.sbuf_tensor("hs_hi", [P, SPLIT_SLOTS, HALF], F32R))
            hs_lo = first.enter_context(nc.sbuf_tensor("hs_lo", [P, SPLIT_SLOTS, HALF], F32R))
            sil = first.enter_context(nc.sbuf_tensor("sil", [P, 2, HALF], F32))
            y_b = first.enter_context(nc.sbuf_tensor("y_b", [P, HT, D], F32))
        with ExitStack() as second:
            qk = second.enter_context(nc.sbuf_tensor("qk", [P, 12, SEQ], F32))
            vT = second.enter_context(nc.sbuf_tensor("vT", [P, 6, SEQ], F32))
        with ExitStack() as third:
            mixT = third.enter_context(nc.sbuf_tensor("mixT", [P, DT, SEQ], F32))
            rows_ = third.enter_context(nc.sbuf_tensor("rows_", [HPG, 2, 2, SEQ], F32))
        sb("region2", [P, 18 * SEQ])
        o_all = vT[:, :, :].rearrange("p t (n e) -> p (t n) e", e=HPG * HEAD)
        junk_sb = sil[:, :, :].rearrange("p a b -> p (a b)")

        ps = ctx.enter_context(nc.psum_tensor("ps", [P, 8, 512], F32))
        junk = ps[:, 6:8, :].rearrange("p a b -> p (a b)")

        w_loaded = [sem(f"w_loaded{n}") for n in range(RAW_SLOTS)]
        hi_done = sem("hi_done")
        lo_done = sem("lo_done")
        used = sem("used")
        sil_done = sem("sil_done")
        h_done = sem("h_done")
        y_act = sem("y_act")
        y_dve = sem("y_dve")
        ident_in = sem("ident_in")
        const_in = sem("const_in")
        w_pool_in = sem("w_pool_in")
        x_last_in = sem("x_last_in")
        y_fin = sem("y_fin")
        g_in = sem("g_in")
        y_in = [sem(f"y_in{n}") for n in range(HT)]
        y_half1_in = sem("y_half1_in")
        sq1_done = sem("sq1_done")
        ms1_done = sem("ms1_done")
        last_scaled = sem("last_scaled")
        last_dve = sem("last_dve")
        last_pool = sem("last_pool")
        last_out = sem("last_out")
        z_done = sem("z_done")
        x_in = sem("x_in")
        xnew_done = sem("xnew_done")
        x_out = sem("x_out")
        sq2_done = sem("sq2_done")
        ms2_done = sem("ms2_done")
        r2_done = sem("r2_done")
        xn_done = sem("xn_done")
        xT_done = sem("xT_done")
        xhi_done = sem("xhi_done")
        xlo_done = sem("xlo_done")
        z_evac = sem("z_evac")
        tr_done = sem("tr_done")
        tr_act = sem("tr_act")
        tr_dve = sem("tr_dve")
        q_zeroed = sem("q_zeroed")
        s_done = sem("s_done")
        biased = sem("biased")
        smax_done = sem("smax_done")
        exp_done = sem("exp_done")
        pT_done = sem("pT_done")
        pT_act = sem("pT_act")
        pT_dve = sem("pT_dve")
        pv_done = sem("pv_done")
        o_done = sem("o_done")
        stat_step = sem("stat_step")
        stat_exp = sem("stat_exp")
        coef_done = sem("coef_done")
        scaled = sem("scaled")
        pool_step = sem("pool_step")
        zeroed = sem("zeroed")

        def wait(eng, s, n):
            if not isinstance(n, int) or n > 0:
                eng.wait_ge(s, n)

        x_in_dram = io["x"]
        JOBS = [
            dict(half=0, y=y, Q0=0), dict(half=1, y=y, Q0=4),
            dict(half=0, y=y, src=x_in_dram, dst=xs1, y0=0, need=4, P0=0, Q0=8),
            dict(half=1, y=y, src=x_in_dram, dst=xs1, y0=4, need=8, P0=4, Q0=12),
            dict(half=0, y=y, src=xs1, dst=xs2, y0=8, P0=8, Q0=16, rows=x_rows, xn=xn_out),
            dict(half=1, y=y_b, src=xs1, dst=xs2, y0=12, need=16, P0=12, Q0=20),
            dict(half=0, y=y, src=xs2, dst=out, y0=16, need=20, P0=16),
        ]
        G_COUNT = [16, 16, 48, 48, 80, 80, 96]
        OUT_SIDE = {7: 0, 10: 1, 13: 2, 16: 3}

        def tr_copied(eng, b):
            on_act = TR_ON_ACT[b]
            eng.wait_ge(tr_act if on_act else tr_dve, sum(1 for a in TR_ON_ACT[:b + 1] if a == on_act))

        def copy_v(copy, b):
            bank = ps[:, TR_BANK[b], :]
            if 4 <= b < 8:
                c = b - 4
                n = 2 if c < 3 else 1
                copy(b, v_mid[:, 2 * c:2 * c + n, :].rearrange("p a b -> p (a b)"), bank[:, 0:n * HPG * HEAD])
            else:
                g, c = (0, b) if b < 4 else ((b - 4) // 4, b % 4)
                copy(b, v_nat[:, g, 2 * c:2 * c + 2, :].rearrange("p a b -> p (a b)"), bank)

        def copy_stat(copy, b):
            g, s, c = 1 if b < TR_POOL else 2, b // 2 % 2, b % 2
            copy(b, natural(rows_[:, g - 1, s, :], g, c), as_permuted(ps[0:HPG, TR_BANK[b], :], g))

        def copy_coef_rows(copy, b):
            g, c = 1 + (b - TR_ROWS) // 2, (b - TR_ROWS) % 2
            copy(b, *own_half(rows_[:, g - 1, 0, :], ps[0:HPG, TR_BANK[b], :], g, c))

        def turned_in(l):
            return TR_O + 2 * (l - 2), TR_O + 2 * (l - 2) + 1

        def copy_o(copy, b):
            g, w, c = (b - TR_O) // 4, (b - TR_O) // 2 % 2, (b - TR_O) % 2
            copy(b, natural(mixT[:, 2 + 2 * g + w, :], g, c), as_permuted(ps[:, TR_BANK[b], :], g))

        def x_parts(i, job, bank):
            return [((slice(None), slice(4 * b, 4 * b + 4), bass.ds(i * P, P)),
                     ps[:, bank + b, :].rearrange("p (a c) -> p a c", a=4)) for b in (0, 1)]

        def x_at(i, job):
            if "rows" in job:
                return job["rows"][:, i, :]
            if "src" in job:
                return x_tile[:, :]
            return y[:, bass.ds(i, 1), :].rearrange("p a b -> p (a b)")

        def mix_y(i):
            return (y, y_b)[i // HT][:, i % HT, :]

        def scale_out(eng, g):
            o = o_all[:, g * NT:(g + 1) * NT, :].rearrange("p n (h e) -> p (n h) e", e=HEAD)
            c = coef[:, g * NT * HPG:(g + 1) * NT * HPG].rearrange("p (a o) -> p a o", o=1)
            return eng.tensor_tensor(o, o, c.to_broadcast([P, NT * HPG, HEAD]), ALU.mult)

        block = ctx.enter_context(nc.Block())

        @block.sync
        def _(sp):
            def load(u0, t, k, dst_cols, src):
                sp.wait_ge(lo_done, t * BLOCK + (u0 + k - RAW_SLOTS + 1 + LO_CREDIT))
                slot = (u0 + k) % RAW_SLOTS
                for cols, s in zip(dst_cols, src):
                    sp.dma_start(cols(raw[:, slot, :]), s).then_inc(w_loaded[slot], 16)

            def columns(w, start, n=P):
                return w.rearrange("(a p) f -> p a f", p=P)[:, :, bass.ds(start, n)]

            def col_tile(ap):
                return ap.rearrange("p (a f) -> p a f", a=DT)

            def gate_up(p, u0):
                gate, up = io[f"w{p}_gate"], io[f"w{p}_up"]

                def tile(t, k):
                    load(u0, t, k, [col_tile], [columns((gate, up)[k % 2], t * 2 * P + k // 2 * P)])

                first = 1 if u0 == 0 else 0
                if first:
                    for k in range(BLOCK):
                        tile(0, k)
                    small_and_second_half()
                with sp.Fori(first, FT // 2) as t:
                    for k in range(BLOCK):
                        tile(t, k)
                for k in range(2):
                    tile(FT // 2, k)
                load(u0, FT // 2, 2, [lambda ap: col_tile(ap)[:, :, 0:TAIL], lambda ap: col_tile(ap)[:, :, TAIL:P]],
                     [columns(gate, FT * P, TAIL), columns(up, FT * P, TAIL)])

            def rows(w, u0, n):
                def tile(t, k):
                    load(u0, t, k, [lambda ap: ap], [w[bass.ds(t * BLOCK * P + k * P, P), :]])

                with sp.Fori(0, n // BLOCK) as t:
                    for k in range(BLOCK):
                        tile(t, k)

            def down_rows(w, u0):
                rows(w, u0, DOWN_UNITS)
                load(u0, DOWN_UNITS // BLOCK, 0, [lambda ap: ap], [w[(FT - 1) * P:FT * P, :]])
                load(u0, DOWN_UNITS // BLOCK, 1, [lambda ap: ap[0:TAIL, :], lambda ap: ap[TAIL:P, :]],
                     [w[FT * P:FF, :], w[FT * P:FF, :]])

            for i in range(HT):
                sp.dma_start(y[:, i, :], io["x"][i * P:(i + 1) * P, :]).then_inc(y_in[i], 16)
                if i == 0:
                    sp.dma_start(ident[:, :], io["ident"]).then_inc(ident_in, 16)

            def small_and_second_half():
                for ap, name in ((edge[:, :, :], "edge"), (pool_scale[:, :], "pool_scale"),
                                 (distance[:, :], "distance")):
                    sp.dma_start(ap, io[name]).then_inc(const_in, 16)
                sp.wait_ge(xn_done, HT)
                sp.dma_start(y[:, :, :], io["x"][HALF:SEQ, :].rearrange("(i p) d -> p i d", p=P))\
                  .then_inc(y_half1_in, 16)

            for p in (0, 1):
                gate_up(1, GU_U0[p])
                down_rows(io["w1_down"], DOWN_U0[p])
            for hf in (0, 1):
                for l, col in enumerate(IN_COLS[hf]):
                    load(IN_U0[hf], 0, l, [col_tile], [columns(io["w_in"], col * P)])
            for n in range(len(OUT_TILES)):
                rows(io["w_out"], OUT_U0 + n * OUT_UNITS, OUT_UNITS)
            for p in (2, 3):
                gate_up(2, GU_U0[p])
                down_rows(io["w2_down"], DOWN_U0[p])
            for i in range(HT):
                if i == 1:
                    sp.wait_ge(last_pool, 1)
                else:
                    sp.wait_ge(last_dve, 1 if i == 0 else i)
                sp.dma_start(out[HALF + i * P:HALF + (i + 1) * P, :], y[:, i, :]).then_inc(last_out, 16)
            sp.wait_ge(last_out, 16 * HT)

        @block.scalar
        def _(act):
            act.sem_inc(z_evac, Z_CREDIT)

            def split(u0, t, k, src=None, ready=None, dst=hs_hi):
                s = (u0 + k) % SPLIT_SLOTS
                act.wait_ge(w_loaded[(u0 + k) % RAW_SLOTS], loaded_count(u0, t, k))
                act.wait_ge(used, t * BLOCK + (u0 + k - SPLIT_SLOTS + 1 + USED_CREDIT))
                w = act.activation(w_hi[:, s, :], raw[:, (u0 + k) % RAW_SLOTS, :], ACT.Copy)
                if src is not None:
                    if ready is not None:
                        act.wait_ge(*ready)
                    w = act.activation(dst[:, s, 0:src.shape[-1]], src, ACT.Copy)
                w.then_inc(hi_done, 1)

            def sq1(i, job, junk=junk):
                if "need" in job:
                    act.wait_ge(y_act, job["need"])
                    act.wait_ge(y_dve, job["need"])
                else:
                    act.wait_ge(y_act, job["y0"] + i + 1)
                    act.wait_ge(y_dve, job["y0"] + i + 1)
                if "Q0" not in job:
                    act.wait_ge(z_done, i + job["P0"])
                act.activation(junk, job["y"][:, bass.ds(i, 1), :].rearrange("p a b -> p (a b)"), ACT.Square,
                               accum_out=ss1[:, 0:1]).then_inc(sq1_done, 1)

            def sq2(i, job, junk=junk, c=0):
                if c == 0:
                    wait(act, ms2_done, i + job["Q0"])
                if "src" in job:
                    act.wait_ge(xnew_done, i + job["P0"] + 1)
                else:
                    act.wait_ge(y_in[i] if job["half"] == 0 else y_half1_in, 16)
                act.activation(junk, x_at(i, job), ACT.Square, accum_out=ss2[:, c:c + 1]).then_inc(sq2_done, 1)

            def x_hi_part(i, job, bank=4):
                act.wait_ge(xT_done, i + job["Q0"] + 1)
                for at, src in x_parts(i, job, bank):
                    a = act.activation(x_hi[job["half"]][at], src, ACT.Copy)
                a.then_inc(xhi_done, 1)

            def silu(u0, t, k, f0, j_par, rows_in=slice(0, P), rows_out=slice(0, P)):
                act.wait_ge(used, t * BLOCK + (u0 + k + 1 + USED_CREDIT))
                act.wait_ge(h_done, t * 2 + (f0 + k // 2 - 1 + H_CREDIT))
                act.activation(sil[rows_out, j_par, :], ps[rows_in, 2 * j_par, :], ACT.Silu).then_inc(sil_done, 1)

            def gate_up(p, side=None):
                u0, f0 = GU_U0[p], NFT * p

                def blk(t, side):
                    for k in range(BLOCK):
                        split(u0, t, k + 2)
                        if side and k == 0 and "src" in side:
                            sq1(t, side)
                        if side and k == 1 and "Q0" in side:
                            sq2(t, side)
                        if k % 2 == 0:
                            silu(u0, t, k, f0, k // 2)
                        if side and k == 2 and "Q0" in side:
                            x_hi_part(t, side)

                with act.Fori(0, HT) as t:
                    blk(t, side)
                with act.Fori(HT, FT // 2) as t:
                    blk(t, None)
                T = FT // 2
                split(u0, T, 2)
                silu(u0, T, 0, f0, 0)
                split(DOWN_U0[p], 0, 0, h_all[:, 0, :], (h_done, f0 + 1 + H_CREDIT))
                silu(u0, T, 2, f0, 1, slice(0, TAIL), slice(TAIL, P))
                split(DOWN_U0[p], 0, 1, h_all[:, 1, :], (h_done, f0 + 2 + H_CREDIT))

            def evac_y(y0, fin0, dst, tiles, last_unit):
                for q, i in enumerate(tiles):
                    if q < len(tiles) - 1:
                        act.wait_ge(y_fin, fin0 + q + 1)
                    else:
                        act.wait_ge(used, last_unit + 1 + USED_CREDIT)
                    act.activation(dst[q], ps[:, 2 * q, :], ACT.Copy).then_inc(y_act, 1)

            def down(p, nxt):
                u0, f0 = DOWN_U0[p], NFT * p

                def sp2(t, k):
                    src = h_all[:, bass.ds(t * BLOCK + k + 2, 1), :].rearrange("p a b -> p (a b)")
                    split(u0, t, k + 2, src, (h_done, t * BLOCK + (f0 + k + 3 + H_CREDIT)))

                with act.Fori(0, DOWN_UNITS // BLOCK - 1) as t:
                    for k in range(BLOCK):
                        sp2(t, k)
                for k in range(BLOCK):
                    sp2(DOWN_UNITS // BLOCK - 1, k)
                if nxt is not None:
                    split(nxt, 0, 0)
                    evac_y(Y0_FFN[p], FIN0_FFN[p], [y[:, i, 0:512] for i in range(HT)], range(HT), u0 + DOWN_UNITS - 1)
                    split(nxt, 0, 1)

            def project_in(hf, side):
                u0 = IN_U0[hf]
                for l in range(IN_UNITS):
                    t, k = l // BLOCK, l % BLOCK
                    if hf == 1:
                        items(SCHEDULE.get((l, "mid"), []))
                    if l + 2 < IN_UNITS:
                        split(u0, 0, l + 2)
                    elif hf == 0:
                        split(IN_U0[1], 0, l + 2 - IN_UNITS)
                    if side and t < HT:
                        if k == 0:
                            sq1(t, side)
                        if k == 1:
                            sq2(t, side)
                        if k == 2:
                            x_hi_part(t, side)
                    act.wait_ge(used, u0 + l + 1 + USED_CREDIT)
                    src, scale = ps[:, l % 2, :], 1.0
                    col = IN_COLS[hf][l]
                    if col < 2:
                        if l == IN_UNITS - 2:
                            act.wait_ge(sq1_done, 2 * HT)
                            act.wait_ge(xnew_done, 2 * HT)
                        dst = u_pad[:, col, PAD + hf * HALF:PAD + (hf + 1) * HALF]
                    else:
                        g, a, e = (col - 2) // 2 % 3, (col - 2) // 6, col % 2
                        if a == 0:
                            scale = QK_SCALE
                        dst = vT[:, 2 * g + e, :] if a == 2 else qk[:, 6 * a + 2 * g + e, :]
                        dst, src = own_half(dst, src, g, hf)
                    act.activation(dst, src, ACT.Copy, scale=scale).then_inc(z_evac, 1)
                    if hf == 1:
                        items(SCHEDULE.get((l, "end"), []))

            def tr_copy(b, dst, src):
                act.wait_ge(tr_done, b + 1)
                act.activation(dst, src, ACT.Copy).then_inc(tr_act, 1)

            def exps(n):
                act.wait_ge(smax_done, n + 1)
                nk = P if n >= 2 * NT else 2 * P
                for h in range(HPG):
                    a = act.activation(probs[:, n % 2, h, 0:nk], probs[:, n % 2, h, 0:nk], ACT.Exp,
                                       bias=m_neg[:, n * HPG + h:n * HPG + h + 1],
                                       accum_out=den[:, n * HPG + h:n * HPG + h + 1])
                a.then_inc(exp_done, 1)

            def items(todo):
                for what, n in todo:
                    if what == "step":
                        if 0 <= n - 2 < 2 * NT:
                            act.wait_ge(pT_done, n - 1)
                            act.activation(probsT[:, n % 2, 0, :], ps[:, 4, :], ACT.Copy).then_inc(pT_act, 1)
                        if n < NTILES:
                            exps(n)
                    elif what == "out":
                        out_split(n)
                    elif what == "pool":
                        tt, c = (n - TR_POOL) // 2, n % 2
                        act.wait_ge(tr_done, n + 1)
                        act.activation(mixT[:, tt, c * HALF:(c + 1) * HALF], ps[:, TR_BANK[n], :], ACT.Copy,
                                       scale=pool_scale[:, tt:tt + 1]).then_inc(tr_act, 1)
                    elif what != "nat" and TR_ON_ACT[n]:
                        (copy_v if what == "v" else copy_stat)(tr_copy, n)

            def copy_turned(l):
                for b in turned_in(l):
                    if TR_ON_ACT[b]:
                        copy_o(tr_copy, b)

            def joint_softmax():
                out_split(1)
                act.wait_ge(stat_step, STAT_EXP)
                e = nat[:, 0, :, :].rearrange("p g n -> p (g n)")
                act.activation(e, e, ACT.Exp).then_inc(stat_exp, 1)
                for b in range(TR_ROWS, TR_COEF):
                    if TR_ON_ACT[b]:
                        copy_coef_rows(tr_copy, b)
                copy_turned(2)
                for l in range(3, OUT_UNITS):
                    copy_turned(l)
                    out_split(l - 1)

            def out_split(n):
                if n < 3 * OUT_UNITS:
                    tiles = OUT_TILES[n // OUT_UNITS]
                    if n < OUT_UNITS:
                        for b in (TR_POOL + 2 * n, TR_POOL + 2 * n + 1) if n < 2 else turned_in(n):
                            tr_copied(act, b)
                    split(OUT_U0, 0, n, mixT[:, n % OUT_UNITS, tiles[0] * P:(tiles[-1] + 1) * P], dst=hs_out[0])
                else:
                    split(OUT_U0, 0, n)

            def project_out():
                for n in range(3 * OUT_UNITS):
                    p = n // OUT_UNITS
                    if n % OUT_UNITS == OUT_UNITS - 1:
                        evac_y(8 + 3 * p, FIN0_OUT[p], [mix_y(i)[:, 0:512] for i in OUT_TILES[p]], OUT_TILES[p],
                               OUT_U0 + n)
                    if n + 2 >= OUT_EARLY:
                        out_split(n + 2)
                    for base, i in OUT_SIDE.items():
                        if n == base:
                            act.wait_ge(sq2_done, JOBS[4]["Q0"] + i)
                            sq1(i, JOBS[4], junk_sb)
                        if n == base + 2:
                            sq2(i, JOBS[4], junk_sb)
                        if n == base + 5:
                            x_hi_part(i, JOBS[4], 6)

            def last_tiles():
                for i in range(HT):
                    if i < HT - 1:
                        act.wait_ge(y_fin, FIN0_FFN[3] + i + 1)
                    else:
                        act.wait_ge(used, UNITS + USED_CREDIT)
                    if i >= 2:
                        act.wait_ge(sq1_done, JOBS[6]["P0"] + HT + i - 1)
                    act.activation((g_pre, xn)[i % 2][:, :], ps[:, 2 * i:2 * i + 2, :].rearrange("p a b -> p (a b)"),
                                   ACT.Square, accum_out=ss1[:, i:i + 1]).then_inc(sq1_done, 1)

            for i in range(HT):
                sq2(i, JOBS[0], h_all[:, 2 * i:2 * i + 2, :].rearrange("p a b -> p (a b)"), i)
            x_hi_part(0, JOBS[0], 0)
            x_hi_part(1, JOBS[0], 2)
            split(GU_U0[0], 0, 0)
            x_hi_part(2, JOBS[0], 4)
            x_hi_part(3, JOBS[0], 6)
            split(GU_U0[0], 0, 1)
            act.wait_ge(xlo_done, HT)
            gate_up(0, JOBS[1])
            down(0, GU_U0[1])
            gate_up(1, JOBS[2])
            down(1, IN_U0[0])
            project_in(0, JOBS[3])
            project_in(1, None)
            items(AFTER_IN)
            joint_softmax()
            project_out()
            act.wait_ge(xlo_done, JOBS[5]["Q0"])
            gate_up(2, JOBS[5])
            down(2, GU_U0[3])
            gate_up(3, JOBS[6])
            down(3, None)
            last_tiles()

        @block.vector
        def _(dve):
            dve.sem_inc(lo_done, LO_CREDIT)
            dve.sem_inc(h_done, H_CREDIT)

            def split(u0, t, k, src=None, parts=(hs_hi, hs_lo), short=False):
                s = (u0 + k) % SPLIT_SLOTS
                dve.wait_ge(hi_done, t * BLOCK + (u0 + k + 1))
                w = dve.tensor_tensor(w_lo[:, s, :], raw[:, (u0 + k) % RAW_SLOTS, :], w_hi[:, s, :].bitcast(F32),
                                      ALU.subtract)
                if short:
                    both = parts[0][TAIL:P, s, :]
                    w = dve.tensor_tensor(both, src[TAIL:P, :], both.bitcast(F32), ALU.subtract)
                elif src is not None:
                    n = src.shape[-1]
                    w = dve.tensor_tensor(parts[1][:, s, 0:n], src, parts[0][:, s, 0:n].bitcast(F32), ALU.subtract)
                w.then_inc(lo_done, 1)

            def x_new(i, job):
                n = i + job["P0"]
                dve.wait_ge(z_done, n + 1)
                dve.wait_ge(x_in, 16 * (job["P0"] + HT) if "rows" in job else n * 16 + 16)
                x = x_at(i, job)
                dve.scalar_tensor_tensor(out=x, in0=job["y"][:, bass.ds(i, 1), :].rearrange("p a b -> p (a b)"),
                                         scalar=r1[:, 0:1], in1=x, op0=ALU.mult, op1=ALU.add)\
                   .then_inc(xnew_done, 1)

            def x_norm(i, job, dst=None, c=0):
                n = i + job["Q0"]
                dve.wait_ge(r2_done, n + 1)
                if dst is None:
                    dst = job.get("xn", xn)[:, :]
                    dve.wait_ge(xT_done, n)
                dve.scalar_tensor_tensor(out=dst, in0=x_at(i, job), scalar=r2[:, c:c + 1], in1=g_pre[:, :],
                                         op0=ALU.mult, op1=ALU.mult).then_inc(xn_done, 1)

            def x_lo_part(i, job, bank=4):
                dve.wait_ge(xhi_done, i + job["Q0"] + 1)
                for at, src in x_parts(i, job, bank):
                    a = dve.tensor_tensor(x_lo[job["half"]][at], src, x_hi[job["half"]][at].bitcast(F32), ALU.subtract)
                a.then_inc(xlo_done, 1)

            def times_up(u0, t, k, f0, j_par, dst, rows=slice(0, P), bank=None):
                dve.wait_ge(used, t * BLOCK + (u0 + k + 1 + USED_CREDIT))
                dve.wait_ge(sil_done, t * 2 + (f0 + k // 2 + 1))
                up = ps[rows, 2 * j_par + 1 if bank is None else bank, :]
                for d in dst:
                    a = dve.tensor_tensor(d, up, sil[rows, j_par, :], ALU.mult)
                a.then_inc(h_done, 1)

            def gate_up(p, side):
                u0, f0 = GU_U0[p], NFT * p

                def blk(t, side):
                    for k in range(BLOCK):
                        split(u0, t, k + 2)
                        if k % 2 == 1:
                            dst = h_all[:, bass.ds(t * 2 + k // 2, 1), :].rearrange("p a b -> p (a b)")
                            times_up(u0, t, k, f0, k // 2, (dst,))
                        if side and k == 0 and "src" in side:
                            x_new(t, side)
                        if side and k == 1 and "Q0" in side:
                            x_norm(t, side)
                        if side and k == 2 and "Q0" in side:
                            x_lo_part(t, side)

                dve.wait_ge(g_in, G_COUNT[JOBS.index(side)])
                with dve.Fori(0, HT) as t:
                    blk(t, side)
                with dve.Fori(HT, FT // 2) as t:
                    blk(t, None)
                T = FT // 2
                split(u0, T, 2)
                split(DOWN_U0[p], 0, 0, h_all[:, 0, :])
                times_up(u0, T, 1, f0, 0, (h_all[:, FT - 1, :],))
                times_up(u0, T, 2, f0, 1, (h_all[0:TAIL, FT, :], h_all[TAIL:P, FT, :]), slice(TAIL, P), bank=2)
                split(DOWN_U0[p], 0, 1, h_all[:, 1, :])

            def evac_y(fin0, dst, last_unit):
                for q, at in enumerate(dst):
                    if q < len(dst) - 1:
                        dve.wait_ge(y_fin, fin0 + q + 1)
                    else:
                        dve.wait_ge(used, last_unit + 1 + USED_CREDIT)
                    dve.tensor_copy(at, ps[:, 2 * q + 1, :]).then_inc(y_dve, 1)

            def down(p, nxt):
                u0 = DOWN_U0[p]
                T = DOWN_UNITS // BLOCK - 1
                with dve.Fori(0, T) as t:
                    for k in range(BLOCK):
                        split(u0, t, k + 2, h_all[:, bass.ds(t * BLOCK + k + 2, 1), :].rearrange("p a b -> p (a b)"))
                for k in range(BLOCK):
                    split(u0, T, k + 2, h_all[:, T * BLOCK + k + 2, :], short=k == BLOCK - 1)
                if nxt is not None:
                    split(nxt, 0, 0)
                    evac_y(FIN0_FFN[p], [y[:, i, 512:1024] for i in range(HT)], u0 + DOWN_UNITS - 1)
                    split(nxt, 0, 1)

            def project_in(hf, side):
                u0 = IN_U0[hf]

                def blk(t, side, last=False):
                    for k in range(BLOCK):
                        if not last or k < 2:
                            split(u0, t, k + 2)
                        else:
                            split(IN_U0[1], 0, k - 2)
                        if side and k == 0:
                            x_new(t, side)
                        if side and k == 1:
                            x_norm(t, side)
                        if side and k == 2:
                            x_lo_part(t, side)

                if hf == 0:
                    with dve.Fori(0, 4) as t:
                        blk(t, side)
                    blk(4, None, True)
                else:
                    dve.wait_ge(x_out, 16 * 2 * HT)
                    dve.wait_ge(const_in, 3 * 16)
                    for l in range(IN_UNITS):
                        items(SCHEDULE.get((l, "mid"), []))
                        if l + 2 < IN_UNITS:
                            split(u0, 0, l + 2)
                        items(SCHEDULE.get((l, "end"), []))

            def tr_copy(b, dst, src):
                dve.wait_ge(tr_done, b + 1)
                dve.tensor_copy(dst, src).then_inc(tr_dve, 1)

            def maxima(n):
                g, T = divmod(n, NT)
                nk = P if g == 2 else 2 * P
                d0 = {0: 0 if T == 0 else 2 if T == NT - 1 else 1, 1: T % 2 * 2, 2: 3}[g] * 2 * P
                dve.wait_ge(s_done, n + 1)
                for h in range(HPG):
                    a = dve.scalar_tensor_tensor(out=probs[:, n % 2, h, 0:nk], in0=distance[:, d0:d0 + nk],
                                                 scalar=-SLOPES[g * HPG + h] * DILATION[g],
                                                 in1=ps[:, s_banks(n) + h % 2, h // 2 * 256:h // 2 * 256 + nk],
                                                 op0=ALU.mult, op1=ALU.add)
                a.then_inc(biased, 1)
                dve.wait_ge(biased, n + 1)
                dve.tensor_reduce(m_neg[:, n * HPG:(n + 1) * HPG], probs[:, n % 2, :, 0:nk], AX.X, ALU.max,
                                  negate=True).then_inc(smax_done, 1)

            def items(todo):
                for what, n in todo:
                    if what == "step":
                        if 0 <= n - 2 < NTILES:
                            dve.wait_ge(pT_done, n - 1)
                            c = 1 if n - 2 < 2 * NT else 0
                            dve.tensor_copy(probsT[:, n % 2, c, :], ps[:, 4 + c, :]).then_inc(pT_dve, 1)
                        if 0 <= n - 3 < NTILES:
                            dve.wait_ge(pv_done, n - 2)
                            dve.tensor_copy(o_all[:, n - 3, :], ps[:, 6, 0:HPG * HEAD]).then_inc(o_done, 1)
                        if n < NTILES:
                            maxima(n)
                    elif what == "out":
                        out_split(n)
                    elif what != "nat" and not TR_ON_ACT[n]:
                        (copy_v if what == "v" else copy_stat)(tr_copy, n)

            def copy_turned(l):
                for b in turned_in(l):
                    if not TR_ON_ACT[b]:
                        copy_o(tr_copy, b)

            def joint_softmax():
                steps = [0]

                def step(ins):
                    steps[0] += 1
                    ins.then_inc(stat_step, 1)

                def all_steps():
                    dve.wait_ge(stat_step, steps[0])

                step(dve.tensor_copy(nat[:, 0, 0, :], m_neg[:, 0:NT * HPG]))
                dve.wait_ge(exp_done, NT)
                step(dve.tensor_copy(nat[:, 1, 0, :], den[:, 0:NT * HPG]))
                dve.wait_ge(tr_done, TR_NAT + 1)
                back = ps[:, TR_BANK[TR_NAT], 0:4 * NT * HPG].rearrange("p (g s n) -> p g s n", g=2, s=2)
                for t in (0, 1):
                    a = dve.tensor_copy(nat[:, t, 1:3, :], back[:, :, t, :])
                    step(a) if t == 0 else a.then_inc(tr_dve, 1)
                tr_copied(dve, TR_NAT)
                all_steps()
                step(dve.tensor_tensor(m_all[:, :], nat[:, 0, 0, :], nat[:, 0, 1, :], ALU.min))
                all_steps()
                step(dve.tensor_tensor(m_all[:, :], m_all[:, :], nat[:, 0, 2, :], ALU.min))
                all_steps()

                def each(ap):
                    return ap.rearrange("p (o n) -> p o n", o=1).to_broadcast([P, NGROUP, NT * HPG])

                step(dve.tensor_tensor(nat[:, 0, :, :], each(m_all[:, :]), nat[:, 0, :, :], ALU.subtract))
                assert steps[0] == STAT_EXP
                out_split(1)
                dve.wait_ge(stat_exp, 1)
                step(dve.tensor_tensor(nat[:, 1, :, :], nat[:, 1, :, :], nat[:, 0, :, :], ALU.mult))
                all_steps()
                step(dve.tensor_tensor(den_sum[:, :], nat[:, 1, 0, :], nat[:, 1, 1, :], ALU.add))
                all_steps()
                step(dve.tensor_tensor(den_sum[:, :], den_sum[:, :], nat[:, 1, 2, :], ALU.add))
                all_steps()
                step(dve.reciprocal(m_all[:, :], den_sum[:, :]))
                all_steps()
                dve.tensor_tensor(nat[:, 0, :, :], nat[:, 0, :, :], each(m_all[:, :]), ALU.mult).then_inc(coef_done, 1)
                dve.wait_ge(coef_done, 1)
                dve.tensor_copy(coef[:, 0:NT * HPG], nat[:, 0, 0, :]).then_inc(coef_done, 1)
                for b in range(TR_ROWS, TR_COEF):
                    if not TR_ON_ACT[b]:
                        copy_coef_rows(tr_copy, b)
                tr_copy(TR_COEF, coef[:, NT * HPG:], ps[:, TR_BANK[TR_COEF], 0:2 * NT * HPG])
                copy_turned(2)
                for l in range(3, OUT_UNITS):
                    copy_turned(l)
                    out_split(l - 1)

            def out_split(n):
                if n < 3 * OUT_UNITS:
                    tiles = OUT_TILES[n // OUT_UNITS]
                    split(OUT_U0, 0, n, mixT[:, n % OUT_UNITS, tiles[0] * P:(tiles[-1] + 1) * P], hs_out)
                else:
                    split(OUT_U0, 0, n)

            def project_out():
                dve.wait_ge(g_in, G_COUNT[4])
                for n in range(3 * OUT_UNITS):
                    p = n // OUT_UNITS
                    if n % OUT_UNITS == OUT_UNITS - 1:
                        evac_y(FIN0_OUT[p], [mix_y(i)[:, 512:1024] for i in OUT_TILES[p]], OUT_U0 + n)
                    if n + 2 >= OUT_EARLY:
                        out_split(n + 2)
                    for base, i in OUT_SIDE.items():
                        if n == base + 1:
                            x_new(i, JOBS[4])
                        if n == base + 2:
                            x_norm(i, JOBS[4])
                        if n == base + 5:
                            x_lo_part(i, JOBS[4], 6)

            def last_tiles():
                dve.wait_ge(x_last_in, 16)
                for i in range(HT):
                    dve.wait_ge(z_done, JOBS[6]["P0"] + HT + i + 1)
                    dve.scalar_tensor_tensor(out=y[:, i, :], in0=ps[:, 2 * i:2 * i + 2, :].rearrange("p a b -> p (a b)"),
                                             scalar=r1[:, i:i + 1], in1=g_post[:, :], op0=ALU.mult, op1=ALU.mult)\
                       .then_inc(last_scaled, 1)
                    if i != 1:
                        dve.wait_ge(last_scaled, i + 1)
                        dve.tensor_tensor(y[:, i, :], y[:, i, :], y_b[:, i, :], ALU.add).then_inc(last_dve, 1)

            dve.wait_ge(g_in, 16)
            first = JOBS[0]
            for i in range(HT):
                x_norm(i, first, y_b[:, i, :], i)
            for i in range(HT):
                x_lo_part(i, first, 2 * i)
            dve.wait_ge(lo_done, LO_CREDIT + 2)
            gate_up(0, JOBS[1])
            down(0, GU_U0[1])
            gate_up(1, JOBS[2])
            down(1, IN_U0[0])
            project_in(0, JOBS[3])
            project_in(1, None)
            items(AFTER_IN)
            joint_softmax()
            project_out()
            gate_up(2, JOBS[5])
            down(2, GU_U0[3])
            gate_up(3, JOBS[6])
            down(3, None)
            last_tiles()

        @block.gpsimd
        def _(pool):
            pool.memset(neg_half[:, :], -0.5).then_inc(zeroed, 1)
            pool.wait_ge(zeroed, 1)

            def rstd(ss, ms, r, ms_done, n, half, c=0):
                f = 4.0 if half else 1.0
                c = slice(c, c + 1)
                pool.tensor_scalar(ms[:, c], ss[:, c], f / D, f * RMS_EPS, ALU.mult, ALU.add).then_inc(ms_done, 1)
                pool.wait_ge(ms_done, n + 1)
                return pool.tensor_tensor(r[:, c], ms[:, c], neg_half[:, :], ALU.pow)

            def tile(i, job):
                if "src" in job:
                    n = i + job["P0"]
                    row = bass.ds(i * P + job["half"] * HALF, P)
                    if "rows" not in job:
                        pool.dma_start(x_tile[:, :], job["src"][row, :]).then_inc(x_in, 16)
                    pool.wait_ge(sq1_done, n + 1)
                    rstd(ss1, ms1, r1, ms1_done, n, job["y0"] in Y0_FFN)
                    yt = job["y"][:, i, :]
                    pool.tensor_tensor(yt, yt, g_post[:, :], ALU.mult).then_inc(z_done, 1)
                    pool.wait_ge(xnew_done, n + 1)
                    pool.dma_start(job["dst"][row, :], x_at(i, job)).then_inc(x_out, 16)
                if "Q0" in job:
                    q = i + job["Q0"]
                    pool.wait_ge(sq2_done, q + 1)
                    rstd(ss2, ms2, r2, ms2_done, q, False).then_inc(r2_done, 1)
                    pool.wait_ge(xn_done, q + 1)
                if "src" in job and "rows" not in job:
                    pool.wait_ge(x_out, n * 16 + 16)

            def gains(post, pre):
                if post:
                    pool.dma_start(g_post[:, :], io[post].to_broadcast([P, D])).then_inc(g_in, 16)
                if pre:
                    pool.dma_start(g_pre[:, :], io[pre].to_broadcast([P, D])).then_inc(g_in, 16)

            def job(n):
                pool.wait_ge(g_in, G_COUNT[n])
                for i in range(HT):
                    tile(i, JOBS[n])

            def pooling():
                n = [0]

                def step(ins):
                    n[0] += 1
                    ins.then_inc(pool_step, 1)
                    pool.wait_ge(pool_step, n[0])

                pool.wait_ge(z_evac, IN_UNITS + 2 + Z_CREDIT)
                END = PAD + SEQ
                step(pool.memset(u_pad[:, :, 0:PAD], 0.0))
                for tt in range(2):
                    src, dst = u_pad[:, tt, :], wins[0][:, :]
                    for lvl in range(2 * tt + 2):
                        w = POOL_WINDOWS[lvl]
                        s = w // 2
                        step(pool.tensor_tensor(dst[:, 0:END - s], src[:, 0:END - s], src[:, s:END], ALU.add))
                        step(pool.tensor_copy(dst[:, END - s:END], src[:, END - s:END]))
                        if lvl >= 2 * tt:
                            rows = slice(lvl % 2 * HEAD, (lvl % 2 + 1) * HEAD)
                            mean, u = dst[rows, PAD - s:END - s], u_pad[rows, tt, PAD:END]
                            step(pool.tensor_scalar(mean, mean, 1.0 / w, None, ALU.mult))
                            step(pool.tensor_tensor(mean[:, 0:PAD], mean[:, 0:PAD], edge[rows, tt, 0:PAD], ALU.mult))
                            step(pool.tensor_tensor(mean[:, SEQ - PAD:SEQ], mean[:, SEQ - PAD:SEQ],
                                                    edge[rows, tt, PAD:2 * PAD], ALU.mult))
                            step(pool.tensor_tensor(u, mean, u, ALU.subtract))
                        src, dst = dst, wins[(lvl + 1) % 2][:, :]
                assert n[0] == POOL_STEPS

            def zero_rows():
                pool.wait_ge(z_evac, IN_UNITS + 2 + 6 * 2 + 2 + Z_CREDIT)
                both = qk[0:HEAD, 4:6, :]
                pool.memset(q_even[HEAD:P, :, :], 0.0).then_inc(q_zeroed, 1)
                pool.tensor_copy(q_even[0:HEAD, :, :], both).then_inc(q_zeroed, 1)
                pool.wait_ge(q_zeroed, 2)
                pool.memset(both, 0.0).then_inc(q_zeroed, 1)

            def pool_weights():
                pool.wait_ge(used, IN_U0[1] + USED_CREDIT)
                pool.memset(sel_w[:, :, :], 0.0).then_inc(zeroed, 1)
                pool.wait_ge(zeroed, 2)
                for n in range(len(POOL_WINDOWS)):
                    a = (n % 2) * HEAD
                    pool.dma_start(sel_w[a:a + HEAD, n // 2, a:a + HEAD], io["w_pool_lin"][n]).then_inc(w_pool_in, 16)

            gains(None, "g_ffn1_pre")
            for i in range(HT):
                pool.wait_ge(sq2_done, i + 1)
                rstd(ss2, ms2, r2, ms2_done, i, False, i).then_inc(r2_done, 1)
            for u in (0, 1):
                pool.wait_ge(hi_done, u + 1)
                pool.tensor_tensor(w_lo[:, u, :], raw[:, u, :], w_hi[:, u, :].bitcast(F32), ALU.subtract)\
                    .then_inc(lo_done, 1)
            pool.wait_ge(xn_done, HT)
            for n in (1, 2, 3):
                if n == 2:
                    gains("g_ffn1_post", "g_mix_pre")
                job(n)
            pool_weights()
            pool.wait_ge(const_in, 3 * 16)
            pooling()
            zero_rows()
            pool.wait_ge(s_done, NTILES)
            gains("g_mix_post", "g_ffn2_pre")
            pool.wait_ge(used, IN_U0[1] + IN_UNITS + USED_CREDIT)
            for i in range(HT):
                pool.dma_start(x_rows[:, i, :], xs1[i * P:(i + 1) * P, :]).then_inc(x_in, 16)
            pool.wait_ge(coef_done, 2)
            scale_out(pool, 0).then_inc(scaled, 1)
            tr_copied(pool, TR_COEF)
            scale_out(pool, 1).then_inc(scaled, 1)
            scale_out(pool, 2).then_inc(scaled, 1)
            job(4)
            pool.wait_ge(x_out, 16 * 3 * HT)
            job(5)
            gains("g_ffn2_post", None)
            pool.dma_start(y_b[:, :, :], xs2[HALF:SEQ, :].rearrange("(i p) d -> p i d", p=P)).then_inc(x_last_in, 16)
            job(6)
            for i in range(HT):
                n = JOBS[6]["P0"] + HT + i
                pool.wait_ge(sq1_done, n + 1)
                rstd(ss1, ms1, r1, ms1_done, n, True, i).then_inc(z_done, 1)
                if i == HT - 1:
                    pool.wait_ge(x_last_in, 16)
                    pool.wait_ge(last_scaled, 2)
                    pool.tensor_tensor(y[:, 1, :], y[:, 1, :], y_b[:, 1, :], ALU.add).then_inc(last_pool, 1)

        @block.tensor
        def _(pe):
            pe.sem_inc(used, USED_CREDIT)

            def split_ready(u0, t, k):
                pe.wait_ge(lo_done, t * BLOCK + (u0 + k + 1 + LO_CREDIT))
                return (u0 + k) % SPLIT_SLOTS

            def weights_by_x(u0, t, k, half, bank, mid=()):
                s = split_ready(u0, t, k)
                hi = w_hi[:, s, :].rearrange("p (a f) -> p a f", a=DT)
                lo = w_lo[:, s, :].rearrange("p (a f) -> p a f", a=DT)
                for a in range(DT):
                    if a == DT // 2:
                        items(mid)
                    pe.matmul(ps[:, bank, :], hi[:, a, :], x_hi[half][:, a, :], start=(a == 0), stop=False)
                    pe.matmul(ps[:, bank, :], hi[:, a, :], x_lo[half][:, a, :], start=False, stop=False)
                    mm = pe.matmul(ps[:, bank, :], lo[:, a, :], x_hi[half][:, a, :], start=False, stop=(a == DT - 1))
                mm.then_inc(used, 1)

            def transposes(i, job, bank=4, src=xn, earlier=1):
                n = i + job["Q0"]
                pe.wait_ge(xn_done, n + 1)
                wait(pe, xlo_done, n + 1 - earlier)
                for a in range(DT):
                    mm = pe.transpose(ps[:, bank + a // 4, a % 4 * P:(a % 4 + 1) * P], src[:, a * P:(a + 1) * P],
                                      ident[:, :])
                mm.then_inc(xT_done, 1)

            def y_banks_free(y0, bank):
                if y0 is not None:
                    pe.wait_ge(y_act if bank % 2 == 0 else y_dve, y0 + bank // 2 + 1)

            def gate_up(p, half, side, d):
                u0, f0 = GU_U0[p], NFT * p

                def unit(t, k, side=None):
                    if k == 3 and side and "Q0" in side:
                        if d is not None and d != Y0_LAST_OUT:
                            y_banks_free(d, 4)
                            y_banks_free(d, 5)
                        transposes(t, side)
                    if k % 2 == 0:
                        pe.wait_ge(h_done, t * 2 + (f0 + k // 2 - 1 + H_CREDIT))
                    y_banks_free(d, k)
                    weights_by_x(u0, t, k, half, k)

                pe.wait_ge(xlo_done, side["Q0"] if "Q0" in side else 24)
                with pe.Fori(0, HT) as t:
                    for k in range(BLOCK):
                        unit(t, k, side)
                with pe.Fori(HT, FT // 2) as t:
                    for k in range(BLOCK):
                        unit(t, k)
                for k in range(3):
                    unit(FT // 2, k)

            def accumulate(u0, t, k, first, last, tiles=ACC_ORDER, after=None, h=(hs_hi, hs_lo), short=False):
                s = split_ready(u0, t, k)
                tiles = sorted(tiles) if last else tiles
                for i in tiles:
                    if after is not None:
                        after(i)
                    hi, lo = (part[:, s, i * P:(i + 1) * P] for part in h)
                    for n in (0, 1):
                        acc, cols = ps[:, 2 * i + n, :], slice(n * 512, (n + 1) * 512)
                        pe.matmul(acc, hi, w_hi[:, s, cols], start=first, stop=False)
                        if short:
                            mm = pe.matmul(acc, hi[0:TAIL, :], w_lo[0:TAIL, s, cols], start=False, stop=last)
                        else:
                            pe.matmul(acc, hi, w_lo[:, s, cols], start=False, stop=False)
                            mm = pe.matmul(acc, lo, w_hi[:, s, cols], start=False, stop=last)
                    if last and i != tiles[-1]:
                        mm.then_inc(y_fin, 1)
                mm.then_inc(used, 1)

            def down(p):
                u0 = DOWN_U0[p]

                def left(i):
                    if i == 0:
                        pe.wait_ge(h_done, NFT * (p + 1) + H_CREDIT)

                for k in range(BLOCK):
                    accumulate(u0, 0, k, k == 0, False, after=left if k == 0 else None)
                with pe.Fori(1, DOWN_UNITS // BLOCK) as t:
                    for k in range(BLOCK):
                        accumulate(u0, t, k, False, False)
                T = DOWN_UNITS // BLOCK
                accumulate(u0, T, 0, False, False)
                accumulate(u0, T, 1, False, True, short=True)

            def project_in(side, d):
                pe.wait_ge(xlo_done, side["Q0"])

                def blk(t, side):
                    for k in range(BLOCK):
                        if side and k == 3:
                            y_banks_free(d, 4)
                            y_banks_free(d, 5)
                            transposes(t, side)
                        y_banks_free(d, k % 2)
                        pe.wait_ge(z_evac, t * BLOCK + (k - 1 + Z_CREDIT))
                        weights_by_x(IN_U0[0], t, k, 0, k % 2)

                with pe.Fori(0, HT) as t:
                    blk(t, side)
                with pe.Fori(HT, IN_UNITS // BLOCK) as t:
                    blk(t, None)

            def project_in_and_attend():
                pe.wait_ge(xlo_done, 16)
                for l in range(IN_UNITS):
                    pe.wait_ge(z_evac, IN_UNITS + l - 1 + Z_CREDIT)
                    weights_by_x(IN_U0[1], 0, l, 1, l % 2, SCHEDULE.get((l, "mid"), []))
                    items(SCHEDULE.get((l, "end"), []))
                items(AFTER_IN)

            def tr_bank(b):
                before = [a for a in range(b) if TR_BANK[a] == TR_BANK[b]]
                if before:
                    tr_copied(pe, before[-1])
                return TR_BANK[b]

            def turn_v(b):
                if b < 4:
                    g, c, off, last = 0, b, 0, 8
                elif b < 8:
                    g, c, off, last = 0, b - 4, SIDE, 8
                else:
                    g, c, off, last = (b - 4) // 4, b % 4, 0, 8 + 6 * ((b - 4) // 4)
                pe.wait_ge(z_evac, IN_UNITS + last + Z_CREDIT)
                if b < 2:
                    pe.wait_ge(pT_dve, 1)
                    pe.wait_ge(pT_act, 1)
                if b == 13:
                    pe.wait_ge(pT_dve, 2 * NT)
                bank = tr_bank(b)
                for e in range(1 if b == 7 else 2):
                    for w in range(2):
                        k0 = (2 * c + e) * P + off
                        mm = pe.transpose(ps[:, bank, (2 * e + w) * P:(2 * e + w + 1) * P],
                                          vT[:, 2 * g + w, k0:k0 + P], ident[:, :])
                mm.then_inc(tr_done, 1)

            def window(n):
                g, T = divmod(n, NT)
                if g == 0:
                    if T == 0:
                        return 0, [v_nat[:, 0, 0, :], v_nat[:, 0, 1, :]]
                    if T == NT - 1:
                        return SEQ - 2 * P, [v_nat[:, 0, NT - 2, :], v_nat[:, 0, NT - 1, :]]
                    return T * P - SIDE, [v_mid[:, T - 1, :], v_mid[:, T, :]]
                if g == 1:
                    a = T // 2 * 2
                    return a * P, [v_nat[:, 1, a, :], v_nat[:, 1, a + 1, :]]
                return T * P, [v_nat[:, 2, T, :]]

            def scores(n):
                g, T = divmod(n, NT)
                k0, vs = window(n)
                nk = len(vs) * P
                pe.wait_ge(z_evac, IN_UNITS + 6 + 6 * g + Z_CREDIT)
                if n == 19:
                    pe.wait_ge(z_evac, 2 * IN_UNITS + Z_CREDIT)
                wait(pe, smax_done, n if n <= 19 else n - 1)
                if g == 2:
                    pe.wait_ge(q_zeroed, 3)
                for h in range(HPG):
                    if g == 2:
                        r, q = slice(0, P), (qk[:, 4 + h // 2, :], q_even[:, h // 2, :])[h % 2 == 0]
                    else:
                        r = slice(h % 2 * HEAD, h % 2 * HEAD + HEAD)
                        q = qk[r, 2 * g + h // 2, :]
                    mm = pe.matmul(ps[:, s_banks(n) + h % 2, h // 2 * 256:h // 2 * 256 + nk], q[:, T * P:(T + 1) * P],
                                   qk[r, 6 + 2 * g + h // 2, k0:k0 + nk], start=True, stop=True)
                mm.then_inc(s_done, 1)

            def turn(n):
                vs = window(n)[1]
                pe.wait_ge(exp_done, n + 1)
                if n >= 1:
                    pe.wait_ge(pT_dve, n)
                    pe.wait_ge(pT_act, min(n, 2 * NT))
                else:
                    pe.wait_ge(xlo_done, 16)
                if n == 1:
                    tr_copied(pe, 4)
                    tr_copied(pe, 5)
                for c in range(len(vs)):
                    for h in range(HPG):
                        mm = pe.transpose(ps[:, 4 + c, h * P:(h + 1) * P], probs[:, n % 2, h, c * P:(c + 1) * P],
                                          ident[:, :])
                mm.then_inc(pT_done, 1)

            def values(n):
                vs = window(n)[1]
                pe.wait_ge(pT_dve, n + 1)
                pe.wait_ge(pT_act, min(n + 1, 2 * NT))
                b = (7, 11, 12 + n % NT // 2)[n // NT]
                tr_copied(pe, b)
                if n < 2 * NT:
                    tr_copied(pe, b - 1)
                if n >= 1:
                    pe.wait_ge(o_done, n)
                for h in range(HPG):
                    for c, v in enumerate(vs):
                        o = h * HEAD
                        mm = pe.matmul(ps[:, 6, o:o + HEAD], probsT[:, n % 2, c, h * P:(h + 1) * P],
                                       v[:, h * HEAD:(h + 1) * HEAD], start=(c == 0), stop=(c == len(vs) - 1))
                mm.then_inc(pv_done, 1)

            def turn_stat(b):
                g, s, c = 1 if b < TR_POOL else 2, b // 2 % 2, b % 2
                pe.wait_ge(exp_done, (g + 1) * NT)
                if b >= TR_STAT2:
                    pe.wait_ge(smax_done, NTILES)
                bank = tr_bank(b)
                for T in range(4):
                    n = (g * NT + 4 * c + T) * HPG
                    mm = pe.transpose(ps[0:HPG, bank, T * P:(T + 1) * P], (m_neg, den)[s][:, n:n + HPG], ident[:, :])
                mm.then_inc(tr_done, 1)

            def items(todo):
                for what, n in todo:
                    if what == "v":
                        turn_v(n)
                    elif what == "stat":
                        turn_stat(n)
                    elif what == "pool":
                        pool_linear(n)
                    elif what == "nat":
                        turn_back(n)
                    elif what == "step":
                        if 0 <= n - 2 < NTILES:
                            turn(n - 2)
                        if 0 <= n - 3 < NTILES:
                            values(n - 3)
                        if n < NTILES:
                            scores(n)

            def pool_linear(b):
                pe.wait_ge(pool_step, POOL_STEPS)
                pe.wait_ge(w_pool_in, 16 * len(POOL_WINDOWS))
                tt, c = (b - TR_POOL) // 2, b % 2
                bank = tr_bank(b)
                pe.matmul(ps[:, bank, :], sel_w[:, tt, :], u_pad[:, tt, PAD + c * HALF:PAD + (c + 1) * HALF],
                          start=True, stop=True).then_inc(tr_done, 1)

            def turn_back(b):
                for a in range(TR_STAT2, TR_NAT):
                    tr_copied(pe, a)
                bank = tr_bank(b)
                for g in range(2):
                    for s in range(2):
                        for j in range(NT):
                            n = ((g * 2 + s) * NT + j) * HPG
                            mm = pe.transpose(ps[:, bank, n:n + HPG], rows_[:, g, s, j * P:(j + 1) * P],
                                              ident[0:HPG, 0:HPG])
                mm.then_inc(tr_done, 1)

            def turn_coefficients():
                pe.wait_ge(coef_done, 1)
                for b in range(TR_ROWS, TR_COEF):
                    g, c = 1 + (b - TR_ROWS) // 2, (b - TR_ROWS) % 2
                    bank = tr_bank(b)
                    if b == TR_ROWS:
                        pe.wait_ge(o_done, NTILES)
                    for j in range(4):
                        n = (4 * c + j) * HPG
                        mm = pe.transpose(ps[0:HPG, bank, j * P:(j + 1) * P], nat[:, 0, g, n:n + HPG], ident[:, :])
                    mm.then_inc(tr_done, 1)
                for b in range(TR_ROWS, TR_COEF):
                    tr_copied(pe, b)
                bank = tr_bank(TR_COEF)
                for g in range(2):
                    for T in range(NT):
                        n = (g * NT + T) * HPG
                        mm = pe.transpose(ps[:, bank, n:n + HPG], rows_[:, g, 0, T * P:(T + 1) * P],
                                          ident[0:HPG, 0:HPG])
                mm.then_inc(tr_done, 1)

            def turn_outputs(l):
                g, w = (l - 2) // 2, l % 2
                pe.wait_ge(scaled, g + 1)
                for c, b in enumerate(turned_in(l)):
                    bank = tr_bank(b)
                    for T in range(4):
                        mm = pe.transpose(ps[:, bank, T * P:(T + 1) * P],
                                          o_all[:, g * NT + 4 * c + T, w * P:(w + 1) * P], ident[:, :])
                    mm.then_inc(tr_done, 1)

            def project_out():
                pe.wait_ge(pT_act, 2 * NT)
                pe.wait_ge(pT_dve, NTILES)
                for n in range(3 * OUT_UNITS):
                    if n == 1:
                        turn_coefficients()
                        turn_outputs(2)
                    if 1 <= n < OUT_UNITS - 2:
                        turn_outputs(n + 2)
                    for base, i in OUT_SIDE.items():
                        if n == base + 6:
                            transposes(i, JOBS[4], 6, xn_out)
                    p, l = n // OUT_UNITS, n % OUT_UNITS

                    def left(i):
                        if p > 0:
                            y_banks_free(8 + 3 * (p - 1), 2 * i)
                            y_banks_free(8 + 3 * (p - 1), 2 * i + 1)

                    accumulate(OUT_U0, 0, n, l == 0, l == OUT_UNITS - 1, range(len(OUT_TILES[p])),
                               after=left if l == 0 else None, h=hs_out)

            pe.wait_ge(ident_in, 16)
            for i in range(HT):
                transposes(i, JOBS[0], 2 * i, y_b[:, i, :], earlier=HT)
            gate_up(0, 0, JOBS[1], None)
            down(0)
            gate_up(1, 1, JOBS[2], Y0_FFN[0])
            down(1)
            project_in(JOBS[3], Y0_FFN[1])
            project_in_and_attend()
            project_out()
            gate_up(2, 0, JOBS[5], Y0_LAST_OUT)
            down(2)
            gate_up(3, 1, JOBS[6], Y0_FFN[2])
            down(3)


def constants():
    q, k2, k1 = np.arange(P)[:, None], np.arange(2 * P)[None, :], np.arange(P)[None, :]
    parts = []
    for off in (0, -SIDE, -P):
        rel = np.abs(off + k2 - q)
        parts.append(np.where(rel <= SIDE, rel, MASKED))
    parts.append(np.where(k1 // HEAD == q // HEAD, np.abs(k1 - q), MASKED))
    edge = np.ones((P, 2, 2 * PAD), np.float32)
    for lvl, w in enumerate(POOL_WINDOWS):
        rows, tt = slice(lvl % 2 * HEAD, (lvl % 2 + 1) * HEAD), lvl // 2
        for t in range(w // 2):
            edge[rows, tt, t] = w / (t + w // 2)
        for t in range(1, w // 2):
            edge[rows, tt, 2 * PAD - t] = w / (w // 2 + t)
    return {"ident": np.eye(P, dtype=np.float32), "distance": np.concatenate(parts, axis=1).astype(np.float32),
            "edge": edge}


def kernel(**inputs):
    import concourse.bacc as bacc
    from concourse.bass_utils import run_bass_kernel_spmd

    nc = bacc.Bacc("TRN2", target_bir_lowering=False, num_devices=1)
    arrays = {}
    for name, a in inputs.items():
        a = np.ascontiguousarray(a)
        if name == "x" or name.startswith("w"):
            a = a[0]
        if name == "pool_scale":
            a = np.ascontiguousarray(a.reshape(2, P).T)
        arrays[name] = a
    arrays.update(constants())
    io = {n: nc.dram_tensor(f"in_{n}_dram", a.shape, F32, kind="ExternalInput").ap() for n, a in arrays.items()}
    out = nc.dram_tensor("out_dram", (SEQ, D), F32, kind="ExternalOutput").ap()
    xs1 = nc.dram_tensor("xs1_dram", (SEQ, D), F32).ap()
    xs2 = nc.dram_tensor("xs2_dram", (SEQ, D), F32).ap()
    layer_program(nc, io, out, xs1, xs2)
    r = run_bass_kernel_spmd(nc, [{f"in_{n}_dram": a for n, a in arrays.items()}], core_ids=[0])
    return r.results[0]["out_dram"].reshape(1, SEQ, D)
```
